# Optimizing a Trainium2 kernel written in Bass

```python
import math
import jax, jax.numpy as jnp
from jax import lax
import numpy as np

D_MODEL = 1024
BATCH = 1
SEQ = 512
DEPTH = 1
DEC_BATCH = 8
DEC_SEQ = 8
PAST_LEN = 1024
PAGE_SIZE = 128

MIX_WIDTH = D_MODEL
ATTN_WIDTH = MIX_WIDTH // 2
LRU_WIDTH = MIX_WIDTH - ATTN_WIDTH
N_HEADS = 4
V_DIM = ATTN_WIDTH // N_HEADS
QK_DIM = V_DIM // 2
N_LRU_BLOCKS = 8
LRU_BLOCK = LRU_WIDTH // N_LRU_BLOCKS
CONV_W = 4
LRU_C = 8.0
IN_WIDTH = 3 * ATTN_WIDTH + 2 * LRU_WIDTH
N_GROUPS = 4
EXPERTS_PER_GROUP = 8
N_EXPERTS = N_GROUPS * EXPERTS_PER_GROUP
TOP_K = 2
D_EXPERT = D_MODEL // 4
Q_BLOCK = 128
LN_EPS = 1e-5
DEEPNORM_ALPHA = (2 * DEPTH) ** 0.25
DEEPNORM_BETA = (8 * DEPTH) ** -0.25

kernel_name = 'hymba_diffattn_rglru_hmoe_step'

F32 = jnp.float32

def _layer_norm(x, g, b):
    xf = x.astype(F32)
    mu = jnp.mean(xf, axis=-1, keepdims=True)
    var = jnp.mean(jnp.square(xf - mu), axis=-1, keepdims=True)
    return ((xf - mu) * lax.rsqrt(var + LN_EPS) * g + b).astype(x.dtype)

def _split_proj(x, w_in):
    B, S, _ = x.shape
    z = x @ w_in
    q, k, v, xl, gl = jnp.split(
        z, [ATTN_WIDTH, 2 * ATTN_WIDTH, 3 * ATTN_WIDTH, 3 * ATTN_WIDTH + LRU_WIDTH], axis=-1)
    q = q.reshape(B, S, N_HEADS, 2, QK_DIM)
    k = k.reshape(B, S, N_HEADS, 2, QK_DIM)
    v = v.reshape(B, S, N_HEADS, V_DIM)
    return q, k, v, xl, gl

def _diff_lambda(lq1, lk1, lq2, lk2, lam_init):
    return (jnp.exp(jnp.sum(lq1.astype(F32) * lk1.astype(F32)))
            - jnp.exp(jnp.sum(lq2.astype(F32) * lk2.astype(F32))) + lam_init)

def _diff_weights(s, lam):
    p = jax.nn.softmax(s, axis=-1)
    return p[:, :, 0] - lam * p[:, :, 1]

def _attn_prompt(q, k, v, lam):
    B, S = q.shape[:2]
    nb = S // Q_BLOCK
    scale = QK_DIM ** -0.5
    qb = q.reshape(B, nb, Q_BLOCK, N_HEADS, 2, QK_DIM).swapaxes(0, 1)
    kpos = jnp.arange(S)
    v32 = v.astype(F32)

    def block(args):
        qi, i = args
        s = jnp.einsum('bqhmd,bkhmd->bhmqk', qi, k).astype(F32) * scale
        qpos = i * Q_BLOCK + jnp.arange(Q_BLOCK)
        mask = kpos[None, :] <= qpos[:, None]
        s = jnp.where(mask, s, -jnp.inf)
        w = _diff_weights(s, lam)
        return jnp.einsum('bhqk,bkhv->bqhv', w, v32)

    o = lax.map(block, (qb, jnp.arange(nb)))
    return o.swapaxes(0, 1).reshape(B, S, N_HEADS, V_DIM)

def _attn_sample(q, k_new, v_new, k_past, v_past, lam):
    Sd = q.shape[1]
    P = k_past.shape[1]
    scale = QK_DIM ** -0.5
    s_past = jnp.einsum('bqhmd,bkhmd->bhmqk', q, k_past).astype(F32) * scale
    s_new = jnp.einsum('bqhmd,bkhmd->bhmqk', q, k_new).astype(F32) * scale
    causal = jnp.tril(jnp.ones((Sd, Sd), dtype=bool))
    s_new = jnp.where(causal, s_new, -jnp.inf)
    w = _diff_weights(jnp.concatenate([s_past, s_new], axis=-1), lam)
    return (jnp.einsum('bhqk,bkhv->bqhv', w[..., :P], v_past.astype(F32))
            + jnp.einsum('bhqk,bkhv->bqhv', w[..., P:], v_new.astype(F32)))

def _head_rmsnorm(o, g, lam_init):
    of = o.astype(F32)
    of = of * lax.rsqrt(jnp.mean(jnp.square(of), axis=-1, keepdims=True) + LN_EPS)
    return of * g * (1.0 - lam_init)

def _causal_conv(x, buf, w, b):
    S = x.shape[1]
    xp = jnp.concatenate([buf.astype(x.dtype), x], axis=1)
    out = b + sum(w[j] * xp[:, j:j + S] for j in range(CONV_W))
    return out, xp[:, -(CONV_W - 1):]

def _linear_combine(c1, c2):
    a1, b1 = c1
    a2, b2 = c2
    return a1 * a2, a2 * b1 + b2

def _recurrent_branch(xl, gl, conv_buf, h0, conv_w, conv_b, w_a, b_a, w_x, b_x, lam_lru):
    xc, new_buf = _causal_conv(xl, conv_buf, conv_w, conv_b)
    B, S, C = xc.shape
    xb = xc.reshape(B, S, N_LRU_BLOCKS, LRU_BLOCK)
    r = jax.nn.sigmoid(jnp.einsum('bshi,hij->bshj', xb, w_a).astype(F32) + b_a).reshape(B, S, C)
    ig = jax.nn.sigmoid(jnp.einsum('bshi,hij->bshj', xb, w_x).astype(F32) + b_x).reshape(B, S, C)
    log_a = -LRU_C * r * jax.nn.softplus(-lam_lru.astype(F32))
    a = jnp.exp(log_a)
    mult = jnp.sqrt(jnp.maximum(-jnp.expm1(2.0 * log_a), 0.0))
    u = mult * ig * xc.astype(F32)
    u = u.at[:, 0].add(a[:, 0] * h0.astype(F32))
    _, h = lax.associative_scan(_linear_combine, (a, u), axis=1)
    y = h * jax.nn.gelu(gl.astype(F32))
    return y.astype(xl.dtype), h[:, -1].astype(xl.dtype), new_buf

def _merge(o_attn, y_lru, w_out):
    B, S = y_lru.shape[:2]
    cat = jnp.concatenate([o_attn.reshape(B, S, ATTN_WIDTH).astype(y_lru.dtype), y_lru], axis=-1)
    return cat @ w_out

def _hier_moe(t, wgr, bgr, wer, ber, wg, wu, wd):
    T = t.shape[0]
    glog = (t @ wgr).astype(F32) + bgr
    gprob = jax.nn.softmax(glog, axis=-1)
    gid = jnp.argmax(glog, axis=-1)
    gw = jnp.take_along_axis(gprob, gid[:, None], axis=-1)[:, 0]
    elog = ((t @ wer).astype(F32) + ber).reshape(T, N_GROUPS, EXPERTS_PER_GROUP)
    within = jnp.take_along_axis(elog, gid[:, None, None], axis=1)[:, 0]
    vals, idx = lax.top_k(within, TOP_K)
    ew = jax.nn.softmax(vals, axis=-1) * gw[:, None]
    eid = gid[:, None] * EXPERTS_PER_GROUP + idx
    comb = jnp.sum(jax.nn.one_hot(eid, N_EXPERTS, dtype=F32) * ew[..., None], axis=1)
    comb = comb.reshape(T, N_GROUPS, EXPERTS_PER_GROUP)
    y = jnp.zeros((T, t.shape[1]), F32)
    for g in range(N_GROUPS):
        sl = slice(g * EXPERTS_PER_GROUP, (g + 1) * EXPERTS_PER_GROUP)
        h = (jax.nn.silu(jnp.einsum('td,edf->tef', t, wg[sl]).astype(F32))
             * jnp.einsum('td,edf->tef', t, wu[sl]).astype(F32))
        y = y + jnp.einsum('tef,efd->td', h * comb[:, g, :, None], wd[sl].astype(F32))
    return y.astype(t.dtype)

def setup_inputs(seed: int = 0) -> dict:
    key = jax.random.key(seed)
    ks = jax.random.split(key, 32)
    n_pages = PAST_LEN // PAGE_SIZE
    n_phys = (5 * DEC_BATCH * n_pages + 3) // 4

    def nrm(k, shape, scale):
        return jax.random.normal(k, shape, F32) * scale

    x_prompt = nrm(ks[0], (BATCH, SEQ, D_MODEL), 1.0)
    x_sample = nrm(ks[1], (DEC_BATCH, DEC_SEQ, D_MODEL), 1.0)
    cache_k = nrm(ks[2], (DEPTH, n_phys, PAGE_SIZE, N_HEADS, 2 * QK_DIM), 1.0)
    cache_v = nrm(ks[3], (DEPTH, n_phys, PAGE_SIZE, N_HEADS, V_DIM), 1.0)
    state_h = nrm(ks[4], (DEPTH, DEC_BATCH, LRU_WIDTH), 0.5)
    state_conv = nrm(ks[5], (DEPTH, DEC_BATCH, CONV_W - 1, LRU_WIDTH), 1.0)
    page_table = jax.random.permutation(ks[6], n_phys)[:DEC_BATCH * n_pages].reshape(
        DEC_BATCH, n_pages).astype(jnp.int32)
    u = jax.random.uniform(ks[7], (DEPTH, LRU_WIDTH), F32, 0.9, 0.999)
    s = u ** (1.0 / LRU_C)
    lru_lambda = jnp.log(s) - jnp.log1p(-s)
    return {
        'x_prompt': x_prompt,
        'x_sample': x_sample,
        'cache_k': cache_k,
        'cache_v': cache_v,
        'state_h': state_h,
        'state_conv': state_conv,
        'page_table': page_table,
        'w_in': nrm(ks[8], (DEPTH, D_MODEL, IN_WIDTH), D_MODEL ** -0.5),
        'lambda_q1': nrm(ks[9], (DEPTH, QK_DIM), 0.1),
        'lambda_k1': nrm(ks[10], (DEPTH, QK_DIM), 0.1),
        'lambda_q2': nrm(ks[11], (DEPTH, QK_DIM), 0.1),
        'lambda_k2': nrm(ks[12], (DEPTH, QK_DIM), 0.1),
        'subln_g': 1.0 + nrm(ks[13], (DEPTH, V_DIM), 0.02),
        'conv_w': nrm(ks[14], (DEPTH, CONV_W, LRU_WIDTH), CONV_W ** -0.5),
        'conv_b': nrm(ks[15], (DEPTH, LRU_WIDTH), 0.02),
        'w_rg_a': nrm(ks[16], (DEPTH, N_LRU_BLOCKS, LRU_BLOCK, LRU_BLOCK), LRU_BLOCK ** -0.5),
        'b_rg_a': nrm(ks[17], (DEPTH, N_LRU_BLOCKS, LRU_BLOCK), 0.1),
        'w_rg_x': nrm(ks[18], (DEPTH, N_LRU_BLOCKS, LRU_BLOCK, LRU_BLOCK), LRU_BLOCK ** -0.5),
        'b_rg_x': nrm(ks[19], (DEPTH, N_LRU_BLOCKS, LRU_BLOCK), 0.1),
        'lru_lambda': lru_lambda,
        'w_out': nrm(ks[20], (DEPTH, MIX_WIDTH, D_MODEL), DEEPNORM_BETA * MIX_WIDTH ** -0.5),
        'ln1_g': 1.0 + nrm(ks[21], (DEPTH, D_MODEL), 0.02),
        'ln1_b': nrm(ks[22], (DEPTH, D_MODEL), 0.02),
        'w_group_router': nrm(ks[23], (DEPTH, D_MODEL, N_GROUPS), D_MODEL ** -0.5),
        'b_group_router': nrm(ks[24], (DEPTH, N_GROUPS), 0.01),
        'w_expert_router': nrm(ks[25], (DEPTH, D_MODEL, N_EXPERTS), D_MODEL ** -0.5),
        'b_expert_router': nrm(ks[26], (DEPTH, N_EXPERTS), 0.01),
        'w_gate_e': nrm(ks[27], (DEPTH, N_EXPERTS, D_MODEL, D_EXPERT), D_MODEL ** -0.5),
        'w_up_e': nrm(ks[28], (DEPTH, N_EXPERTS, D_MODEL, D_EXPERT), D_MODEL ** -0.5),
        'w_down_e': nrm(ks[29], (DEPTH, N_EXPERTS, D_EXPERT, D_MODEL), DEEPNORM_BETA * D_EXPERT ** -0.5),
        'ln2_g': 1.0 + nrm(ks[30], (DEPTH, D_MODEL), 0.02),
        'ln2_b': nrm(ks[31], (DEPTH, D_MODEL), 0.02),
    }

def reference(x_prompt, x_sample, cache_k, cache_v, state_h, state_conv, page_table,
              w_in, lambda_q1, lambda_k1, lambda_q2, lambda_k2, subln_g,
              conv_w, conv_b, w_rg_a, b_rg_a, w_rg_x, b_rg_x, lru_lambda, w_out,
              ln1_g, ln1_b, w_group_router, b_group_router, w_expert_router, b_expert_router,
              w_gate_e, w_up_e, w_down_e, ln2_g, ln2_b):
    xp, xs = x_prompt, x_sample
    Bp, Sp = xp.shape[:2]
    Bd, Sd = xs.shape[:2]
    past = page_table.shape[1] * PAGE_SIZE
    kp_l, vp_l, hp_l, cp_l, ks_l, vs_l, hs_l, cs_l = [], [], [], [], [], [], [], []
    for l in range(DEPTH):
        lam_init = 0.8 - 0.6 * math.exp(-0.3 * l)
        lam = _diff_lambda(lambda_q1[l], lambda_k1[l], lambda_q2[l], lambda_k2[l], lam_init)
        lru_args = (conv_w[l], conv_b[l], w_rg_a[l], b_rg_a[l], w_rg_x[l], b_rg_x[l], lru_lambda[l])

        q, k, v, xl, gl = _split_proj(xp, w_in[l])
        o = _head_rmsnorm(_attn_prompt(q, k, v, lam), subln_g[l], lam_init)
        y_lru, h_last, cbuf = _recurrent_branch(
            xl, gl, jnp.zeros((Bp, CONV_W - 1, LRU_WIDTH), xp.dtype),
            jnp.zeros((Bp, LRU_WIDTH), F32), *lru_args)
        xp = _layer_norm(DEEPNORM_ALPHA * xp + _merge(o, y_lru, w_out[l]), ln1_g[l], ln1_b[l])
        kp_l.append(k.reshape(Bp, Sp, N_HEADS, 2 * QK_DIM))
        vp_l.append(v)
        hp_l.append(h_last)
        cp_l.append(cbuf)

        q, k, v, xl, gl = _split_proj(xs, w_in[l])
        k_past = cache_k[l, page_table].reshape(Bd, past, N_HEADS, 2, QK_DIM)
        v_past = cache_v[l, page_table].reshape(Bd, past, N_HEADS, V_DIM)
        o = _head_rmsnorm(_attn_sample(q, k, v, k_past, v_past, lam), subln_g[l], lam_init)
        y_lru, h_last, cbuf = _recurrent_branch(xl, gl, state_conv[l], state_h[l], *lru_args)
        xs = _layer_norm(DEEPNORM_ALPHA * xs + _merge(o, y_lru, w_out[l]), ln1_g[l], ln1_b[l])
        ks_l.append(k.reshape(Bd, Sd, N_HEADS, 2 * QK_DIM))
        vs_l.append(v)
        hs_l.append(h_last)
        cs_l.append(cbuf)

        tok = jnp.concatenate([xp.reshape(-1, D_MODEL), xs.reshape(-1, D_MODEL)], axis=0)
        f = _hier_moe(tok, w_group_router[l], b_group_router[l], w_expert_router[l],
                      b_expert_router[l], w_gate_e[l], w_up_e[l], w_down_e[l])
        n_p = Bp * Sp
        xp = _layer_norm(DEEPNORM_ALPHA * xp + f[:n_p].reshape(xp.shape), ln2_g[l], ln2_b[l])
        xs = _layer_norm(DEEPNORM_ALPHA * xs + f[n_p:].reshape(xs.shape), ln2_g[l], ln2_b[l])

    return (xp, xs, jnp.stack(kp_l), jnp.stack(vp_l), jnp.stack(hp_l), jnp.stack(cp_l),
            jnp.stack(ks_l), jnp.stack(vs_l), jnp.stack(hs_l), jnp.stack(cs_l))


_drawn_inputs = setup_inputs


def setup_inputs(seed=0):
    import zlib

    import numpy as np

    out = dict(_drawn_inputs(seed))
    spreads = {}
    factors = {'lambda_q1': 5.547,
     'lambda_k1': 8.0,
     'lambda_k2': 22.04,
     'subln_g': 6.102,
     'b_group_router': 20.39,
     'b_expert_router': 8.0,
     'ln2_g': 7.659,
     'ln2_b': 8.009,
     'lambda_q2': 5.511}
    for name, (base, spread) in spreads.items():
        noise = np.random.default_rng([zlib.crc32(name.encode()), seed]).standard_normal(out[name].shape)
        drawn = base * np.exp(spread * noise) if base else spread * noise
        out[name] = __import__('jax').numpy.asarray(drawn.astype(out[name].dtype))
    for name, factor in factors.items():
        out[name] = (out[name] * factor).astype(out[name].dtype)
    return out
```

```python
from contextlib import ExitStack

import concourse.bass as bass
from concourse import mybir

F32, I32 = mybir.dt.float32, mybir.dt.int32
ALU, ACT, AX = mybir.AluOpType, mybir.ActivationFunctionType, mybir.AxisListType

P = 128
D, SEQ, NB, SD, PAST, PAGE = 1024, 512, 8, 8, 1024, 128
NPG = PAST // PAGE
TS = NB * SD
T = SEQ + TS
NT = (T + P - 1) // P
KD = D // P
NH, W = 4, 512
IN_W = 5 * W
NBLK, BLK = 8, 64
HALF = T // 2
XSEG = SEQ + 3
SSEG = SD + 3
XLW = XSEG + NB * SSEG
NG, EPG, NE, FE = 4, 8, 32, 256
CAP = 64
RING = 3
ROUND0 = 6
ROUNDS = 9
NPAIR = RING * ROUNDS + 1
TAB0 = 2 * RING * (ROUND0 - 1)
NEXTRA = 2 * RING * ROUNDS - NE
MOREQ = 8
ALPHA, EPS, LRU_C = 2.0 ** 0.25, 1e-5, 8.0
LAM_INIT = 0.8 - 0.6
NEG = -1e30

GUW, DW = 2 * KD * FE, 2 * D
TILEW = GUW + DW
A_XT = 0
A_V = 0
A_XL = 4608
A_LRU = A_XL + 4 * XLW + 4
A_KT, A_PE, A_PT, A_TMP = 4608, 4608 + 4 * 1152, 4608 + 6 * 1152, 4608 + 7 * 1152
A_VN = 18560
A_BD = A_VN + NT * W
A_STG = A_BD + 2 * 4 * P
A_MSK = A_STG + 4 * W
A_WIN = 2 * 2 * TILEW
A_CAT = A_WIN + 2 * KD * W
A_KN = A_CAT + KD * T
A_QD = A_KN + NH * T
A_MOE = RING * 2 * TILEW
A_X1T = A_MOE
A_QZ = A_QD + NB * NH * 32
A_RT = A_X1T + KD * T
A_X = A_QZ + NH * 2 * SEQ
A_LN = A_X + NT * D
A_SM = A_LN + 2 * D
A_END = 53180


def build(nc, A, O):
    es = ExitStack()
    with es:
        def sem(name):
            return es.enter_context(nc.semaphore(name))

        arena = es.enter_context(nc.sbuf_tensor("arena", [P, A_END], F32))
        ps = es.enter_context(nc.psum_tensor("ps", [P, 8, 512], F32))
        x1_dram = nc.dram_tensor("x1_rows", (T, D), F32, kind="Internal").ap()
        y_slots = nc.dram_tensor("y_slots", (RING * ROUNDS * P, D), F32, kind="Internal").ap()

        def area(at, *dims):
            n = 1
            for d in dims:
                n *= d
            v = arena[:, at:at + n]
            if len(dims) == 2:
                v = v.rearrange("p (a b) -> p a b", b=dims[1])
            if len(dims) == 3:
                v = v.rearrange("p (a b c) -> p a b c", b=dims[1], c=dims[2])
            return v

        top = [A_SM]

        def small(*dims):
            n = 1
            for d in dims:
                n *= d
            at = top[0]
            top[0] += n
            assert top[0] <= A_END, top[0]
            return area(at, *dims)

        rtop = [A_RT]

        def rtemp(*dims):
            n = 1
            for d in dims:
                n *= d
            at = rtop[0]
            rtop[0] += n
            assert rtop[0] <= A_X, rtop[0]
            return area(at, *dims)

        xT = area(A_XT, KD, T)
        win = [area(A_WIN + i * KD * W, KD, W) for i in range(2)]
        xl = area(A_XL, 4, XLW)
        xc, rg, ig, th, hh = [area(A_LRU + i * 4 * T, 4, T) for i in range(5)]
        zeros = area(A_LRU + 16 * T, D)
        bd = area(A_BD, 2, 4, P)
        cat = area(A_CAT, KD, T)
        kTn = area(A_KN, NH, T)
        vn = area(A_VN, NT, W)
        qz = area(A_QZ, NH, 2, SEQ)
        qd = area(A_QD, NB, NH, 32)
        x = area(A_X, NT, D)
        lng, lnb = area(A_LN, D), area(A_LN + D, D)
        kstage = area(A_STG, 2, W)
        rows_in = area(A_STG + 2 * W, W)
        ends_out = area(A_STG + 3 * W, W)
        osb, osq = area(A_STG + 2 * W, NH, P), area(A_STG + 3 * W, NH, P)
        dmask, bigm, sel = area(A_MSK, P), area(A_MSK + P, 184), area(A_MSK + P + 184, 32)
        assert A_MSK + P + 184 + 32 <= A_WIN
        ioti, iotf = area(A_CAT, 184).bitcast(I32), area(A_CAT + 184, 184)
        sel01 = [area(A_CAT + 368 + i * 32, 32) for i in range(2)]
        lamv = area(A_CAT + 432, 4, BLK)
        pexp = [area(A_TMP + i * 2 * SEQ, 2, SEQ) for i in range(2)]
        wdiff = [area(A_TMP + 4 * SEQ + i * SEQ, SEQ) for i in range(2)]
        wT = [area(A_TMP + 6 * SEQ + i * SEQ, SEQ) for i in range(2)]
        assert A_TMP + 8 * SEQ <= A_VN and A_LRU + 20 * T <= A_VN
        kpages = [area(A_WIN + i * NPG * W, NPG, W) for i in range(2)]
        vpages = [area(A_V, NPG, W), area(A_TMP, NPG, W)]
        kT = area(A_KT, NH, 1152)
        pes = [area(A_PE + i * 1152, 9, P) for i in range(2)]
        pT = area(A_PT, 9, P)
        osm = [area(A_STG + i * P, P) for i in range(2)]
        oTs = area(A_STG + W, NB, 32)
        oTq = area(A_STG + 2 * W, NB, 32)
        oTr = area(A_STG + 3 * W, NB, 32)
        wout = area(A_WIN, KD, D)
        x1T = area(A_X1T, KD, T)
        xg = area(A_MOE, D)
        xTm = area(A_MOE + D, KD, P)
        sg = [area(A_MOE + 2 * D + i * P, P) for i in range(2)]
        hid = [area(A_MOE + 2 * D + (2 + i) * P, P) for i in range(2)]
        hT = [area(A_MOE + 2 * D + (4 + i) * P, P) for i in range(2)]
        ysb = [area(A_MOE + 2 * D + 6 * P + i * W, W) for i in range(2)]
        yg = area(0, NT, 2, D)
        ident = small(P)
        qcur = small(NH, 32)
        prm = small(4, 40)
        ends = small(4, 36)
        cl = small(4, 4)
        g08 = small(1)
        lex = small(4, 1)
        parti, partf = small(1).bitcast(I32), small(1)
        sc = small(32)
        mx, sm, rc = small(2, 2), small(2, 2), small(2, 2)
        st = small(12)
        mv = small(NT, 2)
        ss = small(NH)
        coef = small(4)
        ptab = small(64).bitcast(I32)
        info = small(32).bitcast(I32)
        idx = small(NPAIR).bitcast(I32)
        icur = small(1).bitcast(I32)
        yidx = small(2, NT).bitcast(I32)
        wgt = small(2, NT)
        nhalf = small(NT)
        pw = small(NT)

        wr, rbias = rtemp(KD, NG + NE), rtemp(NG + NE)
        ones, tri = rtemp(P), rtemp(P)
        io128i, io128f = rtemp(P).bitcast(I32), rtemp(P)
        toki, tokf, valid = rtemp(NT).bitcast(I32), rtemp(NT), rtemp(NT)
        L = rtemp(NT, NG + NE)
        rexp = rtemp(NT, NG + 1)
        gmax, m1, m2, first = rtemp(NT), rtemp(NT), rtemp(NT), rtemp(NT)
        goh, oh1, oh2, t8, wi = rtemp(NT, NG), rtemp(NT, EPG), rtemp(NT, EPG), rtemp(NT, EPG), rtemp(NT, EPG)
        ek = rtemp(2 * NT, NE)
        ekx = rtemp(2 * NT, NE)
        ohs, rank = rtemp(NT, NE), rtemp(NT, NE)
        run, more, before, upto = rtemp(NE), rtemp(NE), rtemp(NE), rtemp(NE)
        capt, pairt = rtemp(MOREQ), rtemp(NPAIR - 1)
        rk, rb, re_, rf, rs = [rtemp(2 * NT) for _ in range(5)]
        one = rtemp(4)
        lgT = area(A_X1T, T)
        xsel, xsel2 = area(A_X1T + T, NEXTRA, NE), area(A_X1T + T + NEXTRA * NE, NEXTRA, NE)
        at = A_X1T + T + 2 * NEXTRA * NE
        posoh = area(at, 2 * NT, P)
        pairoh = area(at + 2 * NT * P, 2 * NT, NPAIR)
        cmp8 = area(at + 2 * NT * (P + NPAIR), 2 * NT, NPAIR)
        assert at + 2 * NT * (P + 2 * NPAIR) <= A_RT
        assert NE - TAB0 == 2 and RING * (ROUNDS - ROUND0) * 2 + 4 == NEXTRA

        s_x = sem("x_in"); s_win = [sem(f"w_in{i}") for i in range(2)]
        s_par = sem("params_in"); s_bdin = sem("gate_blocks_in"); s_pt = sem("page_table_in")
        s_cst = sem("constants"); s_ln1 = sem("ln1_and_lambdas_in"); s_rt = sem("router_in"); s_lc = sem("late_constants")
        s_le = sem("lru_exp_in"); s_lex = sem("lru_exp"); s_lexp = sem("lambda_exp"); s_mvn = sem("ln_bias"); s_sch = sem("sample_chain"); s_msk = sem("sample_mask"); s_dc = sem("dve_constants")
        s_xtp = sem("x_transposed"); s_xe = [sem(f"xT_half{i}") for i in range(2)]
        s_pj = sem("projected"); s_pev = [sem(f"proj_bank{i}_read") for i in range(2)]
        s_rows = sem("param_rows_transposed"); s_prm = sem("params_ready")
        s_xc = sem("conv_done"); s_lam = sem("lru_rate"); s_gates = sem("gates_act")
        s_th = sem("tanh_done"); s_m2 = sem("mult2_done"); s_mult = sem("mult_done")
        s_ends = sem("ends_ready"); s_endp = sem("ends_transposed"); s_endc = sem("ends_rows")
        s_kt = sem("k_rows_psum"); s_kc = sem("k_rows_sbuf")
        s_kout = [sem(f"k_out{i}") for i in range(2)]
        s_out = sem("small_outputs"); s_ch = sem("dve_chain"); s_pch = sem("pool_chain")
        s_sp = sem("prompt_scores"); s_mxp = sem("prompt_max"); s_exp = sem("prompt_exp")
        s_w = sem("prompt_weights"); s_wt = sem("weights_transposed"); s_wc = sem("wT_ready")
        s_pvp = sem("prompt_values"); s_oc = sem("o_copied"); s_var = sem("rms_in")
        s_rs = sem("rms_out"); s_on = sem("o_normed"); s_ot = sem("o_transposed"); s_oe = sem("o_in_cat")
        s_kin = [sem(f"keys_in{i}") for i in range(2)]; s_vin = [sem(f"values_in{i}") for i in range(2)]
        s_ktp = [sem(f"keys_transposed{i}") for i in range(2)]
        s_ktc = [sem(f"kT_bank{i}_read") for i in range(2)]
        s_qc = sem("query_block"); s_sc = sem("sample_scores"); s_mxs = sem("sample_max")
        s_exs = sem("sample_exp"); s_ptp = sem("probs_transposed"); s_pta = sem("pT_by_act"); s_ptd = sem("pT_by_dve")
        s_pvs = sem("sample_values"); s_os = sem("o_scaled"); s_cmb = sem("maps_combined"); s_oct = sem("combined_read")
        s_sq = sem("o_squared"); s_sqm = sem("square_sums"); s_srs = sem("sample_rms"); s_cat = sem("cat_done")
        s_wo = sem("w_out_in"); s_op = sem("merged"); s_opr = sem("merge_bank_read")
        s_mv = sem("ln_stats"); s_rstd = sem("ln_rstd"); s_nrm = sem("ln_scaled"); s_x1 = sem("x1_ready")
        s_x1d = sem("x1_stored"); s_x1t = sem("x1_transposed"); s_x1e = [sem(f"x1T_half{i}") for i in range(2)]
        s_lg = sem("logits_T"); s_lgc = sem("logits_T_copied"); s_lgt = sem("logits_psum")
        s_ln2 = sem("ln2_params_in")
        s_re = sem("route_exp_in"); s_rx = sem("route_exp"); s_oh = sem("choice_onehots"); s_rk = sem("ranks_psum")
        s_ab = sem("slot_onehots"); s_tab = sem("slot_table_psum"); s_info = sem("routing_done")
        s_wgu = [[sem(f"w_gate_up{i}_{u}") for u in range(2)] for i in range(RING)]
        s_wd = [[sem(f"w_down{i}_{u}") for u in range(2)] for i in range(RING)]
        s_gi = sem("gather_index"); s_gx = sem("rows_gathered"); s_xt = sem("rows_transposed")
        s_xa = sem("xTm_half0"); s_xd = sem("xTm_half1")
        s_gu = [sem(f"gate_up{i}") for i in range(2)]; s_sg = [sem(f"silu{i}") for i in range(2)]
        s_h = [sem(f"hidden{i}") for i in range(2)]; s_ht = [sem(f"hidden_T{i}") for i in range(2)]
        s_hc = [sem(f"hT_ready{i}") for i in range(2)]; s_y = [sem(f"down{i}") for i in range(2)]
        s_yc = [sem(f"y_copied{i}") for i in range(2)]; s_yd = [sem(f"y_stored{i}") for i in range(2)]
        s_xs = sem("x1_scaled")
        s_yg = [sem(f"y_gathered{i}") for i in range(NT)]
        s_mv2 = sem("ln2_stats"); s_rstd2 = sem("ln2_rstd"); s_nrm2 = sem("ln2_scaled"); s_g2 = sem("ln2_gained")
        s_turn = sem("pool_turns"); s_sturn = sem("sync_turns"); s_zero = sem("zeros"); s_fill = sem("spare_slots_filled")
        s_fin = sem("result_ready"); s_res = sem("result_stored")

        def rows(t):
            return P if t < NT - 1 else TS

        XL, GL, Q, K_, V_ = 3, 4, 0, 1, 2
        ORDER = [XL, GL, Q, K_, V_]
        w_in = A["w_in"][0]

        block = es.enter_context(nc.Block())

        @block.sync
        def _(sp):
            sp.dma_start(x[:, 0:NT - 1, :], A["x_prompt"][0].rearrange("(t p) d -> p t d", p=P)).then_inc(s_x, 16)
            sp.dma_start(x[0:TS, NT - 1, :], A["x_sample"].rearrange("b s d -> (b s) d")).then_inc(s_x, 16)
            for n, c in enumerate(ORDER):
                if n >= 2:
                    sp.wait_ge(s_pj, [4, 8, 20][n - 2])
                sp.dma_start(win[n % 2][:, :, :], w_in[:, c * W:(c + 1) * W].rearrange("(k p) n -> p k n", p=P)).then_inc(s_win[n % 2], 16)

            ck = A["cache_k"][0].rearrange("n s h d -> (n s) (h d)")
            n_phys = A["cache_k"].shape[1]
            sp.wait_ge(s_pt, 16)

            def keys(b, u, ready):
                at = [sp.value_load(ptab[0:1, bass.ds(b * NPG + g, 1)], min_val=0, max_val=n_phys - 1) for g in range(NPG)]
                ready()
                for g in range(NPG):
                    sp.dma_start(kpages[u][:, g, :], ck[bass.ds(at[g] * PAGE, PAGE), :]).then_inc(s_kin[u], 16)

            keys(0, 0, lambda: sp.wait_ge(s_pj, 29))
            keys(1, 1, lambda: None)
            with sp.Fori(1, NB // 2) as jb:
                for u in range(2):
                    b = 2 * jb + u

                    def keys_free():
                        sp.wait_ge(s_ktp[1], 4 * b - 4)
                        sp.sem_inc(s_sturn, 1)

                    keys(b, u, keys_free)

            sp.wait_ge(s_ktp[1], 4 * NB)
            sp.dma_start(wout[:, :, :], A["w_out"][0].rearrange("(k p) n -> p k n", p=P)).then_inc(s_wo, 16)

            wg = A["w_gate_e"][0].rearrange("e d f -> (e d) f")
            wu = A["w_up_e"][0].rearrange("e d f -> (e d) f")
            wd = A["w_down_e"][0].rearrange("e f d -> (e f) d")

            def weights(e, slot, u):
                gate, up, down = slot * 2 * TILEW + u * TILEW, slot * 2 * TILEW + u * TILEW + GUW // 2, slot * 2 * TILEW + u * TILEW + GUW
                sp.dma_start(arena[:, gate:up], wg[bass.ds(e * D, D), :].rearrange("(p k) f -> p (k f)", p=P)).then_inc(s_wgu[slot][u], 16)
                sp.dma_start(arena[:, up:down], wu[bass.ds(e * D, D), :].rearrange("(p k) f -> p (k f)", p=P)).then_inc(s_wgu[slot][u], 16)
                sp.dma_start(area(down, 2, D), wd[bass.ds(e * FE, FE), :].rearrange("(a p) d -> p a d", p=P)).then_inc(s_wd[slot][u], 16)

            sp.wait_ge(s_cat, 1)
            sp.wait_ge(s_out, 16 * 6)
            sp.wait_ge(s_kout[0], 16 * 3)
            sp.wait_ge(s_kout[1], 16 * 2)
            for slot in range(RING):
                if slot == RING - 1:
                    sp.wait_ge(s_op, NT)
                for u in range(2):
                    weights(2 * slot + u, slot, u)

            def next_round(r, expert):
                for slot in range(RING):
                    sp.wait_ge(s_y[1], RING * r + slot - (RING - 1))
                    sp.sem_inc(s_sturn, 1)
                    for u in range(2):
                        weights(expert(slot, u), slot, u)

            with sp.Fori(1, ROUND0 - 1) as r:
                next_round(r, lambda slot, u: 2 * RING * r + 2 * slot + u)
            sp.wait_ge(s_info, 1)
            rounds = sp.value_load(info[0:1, 0:1], min_val=ROUND0, max_val=ROUNDS)
            with sp.Fori(ROUND0 - 1, rounds) as r:
                next_round(r, lambda slot, u: sp.value_load(
                    info[0:1, bass.ds(2 * RING * (r - (ROUND0 - 1)) + 2 * slot + u + 1, 1)], min_val=0, max_val=NE - 1))

            for t in range(NT):
                sp.wait_ge(s_fin, t + 1)
                if t < NT - 1:
                    sp.dma_start(O["y_prompt"][0, t * P:(t + 1) * P, :], x[:, t, :]).then_inc(s_res, 16)
                else:
                    sp.dma_start(O["y_sample"].rearrange("b s d -> (b s) d"), x[0:TS, t, :]).then_inc(s_res, 16)
            sp.wait_ge(s_res, 16 * NT)

        @block.gpsimd
        def _(q):
            def pool_link(ins, state=[0]):
                state[0] += 1
                ins.then_inc(s_pch, 1)
                q.wait_ge(s_pch, state[0])

            g = nc.gpsimd
            pool_link(g.memset(ident, 0.0))
            g.affine_select(out=ident, in_=ident, compare_op=ALU.not_equal, fill=1.0, base=0,
                            pattern=[[-1, P]], channel_multiplier=1).then_inc(s_cst, 1)
            g.memset(rows_in, 0.0).then_inc(s_cst, 1)
            q.wait_ge(s_cst, 2)
            q.dma_start(rows_in[0:4, :], A["conv_w"][0]).then_inc(s_par, 16)
            for at, name in ((4, "conv_b"), (7, "lru_lambda")):
                q.dma_start(rows_in[at:at + 1, :], A[name][0:1, :]).then_inc(s_par, 16)
            for at, name in ((5, "b_rg_a"), (6, "b_rg_x")):
                q.dma_start(rows_in[at:at + 1, :], A[name].rearrange("o n b -> o (n b)")).then_inc(s_par, 16)
            q.dma_start(rows_in[8:16, :], A["state_h"][0]).then_inc(s_par, 16)
            q.dma_start(rows_in[16:40, :], A["state_conv"][0].rearrange("b j c -> (b j) c")).then_inc(s_par, 16)
            pool_link(g.memset(bd, 0.0))
            g.memset(zeros, 0.0).then_inc(s_zero, 1)
            for n, name in enumerate(("w_rg_a", "w_rg_x")):
                src = A[name][0].rearrange("(t u) i j -> u i t j", u=2)
                for u in range(2):
                    q.dma_start(bd[u * BLK:(u + 1) * BLK, n, :, u * BLK:(u + 1) * BLK], src[u]).then_inc(s_bdin, 16)
            pool_link(g.memset(qd, 0.0))
            pool_link(g.memset(qz, 0.0))
            pool_link(g.memset(xl[:, :, 0:3], 0.0))
            pool_link(g.memset(vn[:, NT - 1, :], 0.0))
            pool_link(g.memset(dmask, 0.0))
            pool_link(g.affine_select(out=dmask, in_=dmask, compare_op=ALU.is_ge, fill=NEG, base=0,
                                      pattern=[[-1, P]], channel_multiplier=1))
            for m, s in enumerate(sel01):
                pool_link(g.memset(s, 0.0))
                v = s.rearrange("p (h q) -> p h q", q=SD)
                pool_link(g.affine_select(out=v, in_=v, compare_op=ALU.not_equal, fill=1.0, base=-SD * m,
                                          pattern=[[-32, NH], [-1, SD]], channel_multiplier=1))
            pool_link(g.iota(ioti, pattern=[[1, 184]], base=-56, channel_multiplier=0))
            pool_link(g.iota(parti, pattern=[[0, 1]], base=0, channel_multiplier=1))
            g.memset(nhalf, -0.5).then_inc(s_cst, 1)

            cv = A["cache_v"][0].rearrange("n s h d -> (n s) (h d)")
            n_phys = A["cache_v"].shape[1]

            def values(b, u, ready):
                at = [q.value_load(ptab[0:1, bass.ds(b * NPG + g, 1)], min_val=0, max_val=n_phys - 1) for g in range(NPG)]
                ready()
                for g_ in range(NPG):
                    q.dma_start(vpages[u][:, g_, :], cv[bass.ds(at[g_] * PAGE, PAGE), :]).then_inc(s_vin[u], 16)

            for t in range(NT):
                q.wait_ge(s_kc, t + 1)
                if t < NT - 1:
                    dst = O["k_prompt"][0, 0, t * P:(t + 1) * P].rearrange("s h d -> s (h d)")
                else:
                    dst = O["k_sample"][0].rearrange("b s h d -> (b s) (h d)")
                q.dma_start(dst, kstage[0:rows(t), t % 2, :]).then_inc(s_kout[t % 2], 16)
            q.wait_ge(s_pev[0], 30)
            q.wait_ge(s_pev[1], 28)
            q.dma_start(O["v_prompt"][0, 0].rearrange("(t p) h d -> p t (h d)", p=P), vn[:, 0:NT - 1, :]).then_inc(s_out, 16)
            q.dma_start(O["v_sample"][0].rearrange("b s h d -> (b s) (h d)"), vn[0:TS, NT - 1, :]).then_inc(s_out, 16)
            q.wait_ge(s_pt, 16)
            values(0, 0, lambda: q.wait_ge(s_pj, 29))
            q.wait_ge(s_endc, 1)
            q.dma_start(O["h_prompt"][0], ends_out[0:1, :]).then_inc(s_out, 16)
            q.dma_start(O["h_sample"][0], ends_out[1:9, :]).then_inc(s_out, 16)
            q.dma_start(O["conv_prompt"][0, 0], ends_out[9:12, :]).then_inc(s_out, 16)
            q.dma_start(O["conv_sample"][0].rearrange("b j c -> (b j) c"), ends_out[12:36, :]).then_inc(s_out, 16)

            for i in range(NT - 1):
                q.wait_ge(s_var, i + 1)
                g.tensor_tensor(ss, ss, nhalf[:, 0:NH], ALU.pow).then_inc(s_rs, 1)

            def query(b):
                q.wait_ge(s_sc, b)
                q.wait_ge(s_cst, 3)
                g.tensor_copy(qcur, qd[:, b, :, :] if isinstance(b, int) else
                              arena[:, bass.ds(A_QD + b * (NH * 32), NH * 32)].rearrange("p (h c) -> p h c", h=NH)).then_inc(s_qc, 1)

            q.wait_ge(s_sp, 4 * (NT - 1))
            g.memset(ones, 1.0).then_inc(s_lc, 1)
            g.memset(tri, 1.0).then_inc(s_lc, 1)
            q.wait_ge(s_lc, 2)
            g.affine_select(out=tri, in_=tri, compare_op=ALU.is_gt, fill=0.0, base=0, pattern=[[1, P]], channel_multiplier=-1).then_inc(s_lc, 1)
            g.iota(io128i, pattern=[[1, P]], base=0, channel_multiplier=0).then_inc(s_lc, 1)
            g.iota(toki, pattern=[[P, NT]], base=0, channel_multiplier=1).then_inc(s_lc, 1)
            g.tensor_copy(qcur, qd[:, 0, :, :]).then_inc(s_qc, 1)
            values(1, 1, lambda: q.wait_ge(s_pvp, NH * (NT - 1)))
            query(1)
            with q.Fori(1, NB // 2) as jb:
                for u in range(2):
                    b = 2 * jb + u

                    def values_free():
                        q.wait_ge(s_pvs, b - 1)
                        q.sem_inc(s_turn, 1)

                    values(b, u, values_free)
                    query(b)

            for t in range(NT):
                q.wait_ge(s_mv, t + 1)
                g.tensor_tensor(pw[:, t:t + 1], pw[:, t:t + 1], nhalf[:, 0:1], ALU.pow).then_inc(s_rstd, 1)

            q.wait_ge(s_info, 1)
            rounds = q.value_load(info[0:1, 0:1], min_val=ROUND0, max_val=ROUNDS)
            pairs = q.snap(rounds * RING)
            q.wait_ge(s_x1d, 16 * NT)

            def gather(j):
                g.tensor_copy(icur, idx[:, bass.ds(j, 1)]).then_inc(s_gi, 1)
                q.wait_ge(s_gi, j + 1)
                q.sem_inc(s_turn, 1)
                q.indirect_dma_start(out=xg, out_offset=None, in_=x1_dram,
                                     in_offset=bass.IndirectOffsetOnAxis(ap=icur, axis=0)).then_inc(s_gx, 16)

            gather(0)
            with q.Fori(0, pairs) as j:
                q.wait_ge(s_xt, 2 * j + 2)
                q.wait_ge(s_gx, 16 * j + 16)
                q.wait_ge(s_info, 1)
                gather(j + 1)
            q.wait_ge(s_gx, 16 * pairs + 16)

            q.wait_ge(s_fill, 16 * RING * (ROUNDS - ROUND0))
            q.wait_ge(s_yd[0], 32 * pairs)
            q.wait_ge(s_yd[1], 32 * pairs)
            q.sem_inc(s_turn, 1)
            for t in range(NT):
                r = rows(t)
                for k in range(2):
                    q.indirect_dma_start(out=yg[0:r, t, k, :], out_offset=None, in_=y_slots,
                                         in_offset=bass.IndirectOffsetOnAxis(ap=yidx[0:r, k, t:t + 1], axis=0)).then_inc(s_yg[t], 16)
            for t in range(NT):
                r = rows(t)
                q.wait_ge(s_mv2, t + 1)
                g.tensor_tensor(pw[:, t:t + 1], pw[:, t:t + 1], nhalf[:, 0:1], ALU.pow).then_inc(s_rstd2, 1)
                if t:
                    q.wait_ge(s_g2, t)
                    g.tensor_tensor(x[0:rows(t - 1), t - 1, :], x[0:rows(t - 1), t - 1, :], lnb[0:rows(t - 1), :], ALU.add).then_inc(s_fin, 1)
            q.wait_ge(s_g2, NT)
            g.tensor_tensor(x[0:TS, NT - 1, :], x[0:TS, NT - 1, :], lnb[0:TS, :], ALU.add).then_inc(s_fin, 1)

        def o_transpose(pe, i):
            pe.wait_ge(s_on, i + 1)
            if i:
                pe.wait_ge(s_oe, i)
            for h in range(NH):
                last = nc.tensor.transpose(ps[:, 7, h * P:(h + 1) * P], osb[:, h, :], ident)
            last.then_inc(s_ot, 1)

        @block.tensor
        def _(pe):
            mm, tr = nc.tensor.matmul, nc.tensor.transpose
            pe.wait_ge(s_cst, 1)
            pe.wait_ge(s_x, 32)
            for t in range(NT):
                for half in range(2):
                    n = 2 * t + half
                    if n >= 2:
                        pe.wait_ge(s_xe[half], t)
                    for kk in range(4):
                        k = 4 * half + kk
                        last = tr(ps[:, 4 + half, kk * P:kk * P + rows(t)], x[0:rows(t), t, k * P:(k + 1) * P], ident[0:rows(t), 0:rows(t)])
                    last.then_inc(s_xtp, 1)
            pe.wait_ge(s_par, 16 * 7)
            for t in range(4):
                last = tr(ps[:, 6, t * 40:(t + 1) * 40], rows_in[0:40, t * P:(t + 1) * P], ident[0:40, 0:40])
            last.then_inc(s_rows, 1)
            for h in range(2):
                pe.wait_ge(s_xe[h], NT)

            unit = [0]

            def bank_free():
                n = unit[0]
                unit[0] += 1
                if n >= 2:
                    pe.wait_ge(s_pev[n % 2], 2 * (n // 2))
                return 2 * (n % 2)

            def k_rows(t):
                if t >= 2:
                    pe.wait_ge(s_kc, t - 1)
                for h in range(NH):
                    last = tr(ps[0:rows(t), 4 + t % 2, h * P:(h + 1) * P], kTn[:, h, t * P:t * P + rows(t)], ident)
                last.then_inc(s_kt, 1)

            for n, c in enumerate(ORDER):
                pe.wait_ge(s_win[n % 2], 16 * (n // 2 + 1))
                if c != V_:
                    for m in range(4):
                        b = bank_free()
                        for k in range(KD):
                            for h in range(2):
                                last = mm(ps[:, b + h, 0:HALF], win[n % 2][:, k, m * P:(m + 1) * P], xT[:, k, h * HALF:(h + 1) * HALF],
                                          start=k == 0, stop=k == KD - 1)
                        last.then_inc(s_pj, 1)
                else:
                    for t in range(NT):
                        b = bank_free()
                        for k in range(KD):
                            last = mm(ps[0:rows(t), b, :], xT[:, k, t * P:t * P + rows(t)], win[n % 2][:, k, :],
                                      start=k == 0, stop=k == KD - 1)
                        last.then_inc(s_pj, 1)
                if c == GL:
                    pe.wait_ge(s_bdin, 64)
                    for t in range(4):
                        pe.wait_ge(s_xc, t + 1)
                        for a in range(2):
                            b = bank_free()
                            for h in range(2):
                                last = mm(ps[:, b + h, 0:HALF], bd[:, a, t, :], xc[:, t, h * HALF:(h + 1) * HALF], start=True, stop=True)
                            last.then_inc(s_pj, 1)
            for h in range(2):
                pe.wait_ge(s_pev[h], 30 - 2 * h)
            for t in range(NT):
                k_rows(t)
            pe.wait_ge(s_ends, 1)
            for t in range(4):
                last = tr(ps[0:36, 6, t * P:(t + 1) * P], ends[:, t, :], ident)
            last.then_inc(s_endp, 1)

            pe.wait_ge(s_kc, NT)
            pe.wait_ge(s_endc, 1)
            steps = [(i, h) for i in range(NT - 1) for h in range(NH)]

            def scores(n):
                i, h = steps[n]
                if n >= 2:
                    pe.wait_ge(s_exp, n - 1)
                for m in range(2):
                    last = mm(ps[:, 2 * (n % 2) + m, 0:(i + 1) * P], qz[:, h, m, i * P:(i + 1) * P], kTn[:, h, 0:(i + 1) * P], start=True, stop=True)
                last.then_inc(s_sp, 1)

            def transposes(n):
                i, h = steps[n]
                pe.wait_ge(s_w, n + 1)
                if n >= 2:
                    pe.wait_ge(s_wc, n - 1)
                for kt in range(i + 1):
                    last = tr(ps[:, 4 + n % 2, kt * P:(kt + 1) * P], wdiff[n % 2][:, kt * P:(kt + 1) * P], ident)
                last.then_inc(s_wt, 1)

            def values(n):
                i, h = steps[n]
                pe.wait_ge(s_wc, n + 1)
                if h == 0 and i:
                    pe.wait_ge(s_oc, i)
                for kt in range(i + 1):
                    last = mm(ps[:, 6, h * P:(h + 1) * P], wT[n % 2][:, kt * P:(kt + 1) * P], vn[:, kt, h * P:(h + 1) * P],
                              start=kt == 0, stop=kt == i)
                last.then_inc(s_pvp, 1)

            scores(0)
            scores(1)
            transposes(0)
            scores(2)
            for n, (i, h) in enumerate(steps):
                if n + 1 < len(steps):
                    transposes(n + 1)
                values(n)
                if n + 3 < len(steps):
                    scores(n + 3)
                if h == 2 and i:
                    o_transpose(pe, i - 1)
            o_transpose(pe, NT - 2)

            pe.wait_ge(s_oe, NT - 1)
            pe.wait_ge(s_exp, len(steps))
            pe.wait_ge(s_wc, len(steps))

            def keys_transpose(b, u, g, first=False):
                if g == 0:
                    pe.wait_ge(s_kin[u], (b - u) * (P // 2) + P)
                if not (first and g < 2):
                    pe.wait_ge(s_ktc[g % 2], 4 * b + g // 2)
                for h in range(NH):
                    last = tr(ps[:, 3 + g % 2, h * P:(h + 1) * P], kpages[u][:, g, h * P:(h + 1) * P], ident)
                last.then_inc(s_ktp[g % 2], 1)

            def sample_scores(b):
                pe.wait_ge(s_qc, b + 1)
                pe.wait_ge(s_ktc[0], 4 * b + 4)
                pe.wait_ge(s_ktc[1], 4 * b + 4)
                pe.wait_ge(s_exs, b)
                pe.wait_ge(s_cst, 3)
                for c in range(3):
                    for h in range(NH):
                        last = mm(ps[32 * h:32 * h + 32, c, 0:384], qcur[:, h, :], kT[:, h, c * 384:(c + 1) * 384], start=True, stop=True)
                last.then_inc(s_sc, 1)

            def probs_transpose(b, u, grp):
                k0, k1 = ((0, 4), (4, 8), (8, 9))[grp]
                if grp == 0:
                    pe.wait_ge(s_exs, b + 1)
                if grp == 2:
                    pe.wait_ge(s_pta, 2 * b + 1)
                for kt in range(k0, k1):
                    last = tr(ps[:, 5 + grp % 2, (kt - k0) * P:(kt - k0 + 1) * P], pes[u][:, kt, :], ident)
                last.then_inc(s_ptp, 1)

            def sample_values(b, u, k0, k1):
                if k0 == 0:
                    pe.wait_ge(s_vin[u], (b - u) * (P // 2) + P)
                    pe.wait_ge(s_pta, 2 * b + 2)
                    pe.wait_ge(s_ptd, b + 1)
                for kt in range(k0, k1):
                    for h in range(NH):
                        v = vpages[u][:, kt, h * P:(h + 1) * P] if kt < 8 else vn[:, NT - 1, h * P:(h + 1) * P]
                        last = mm(ps[32 * h:32 * h + 32, 7, 0:P], pT[:, kt, 32 * h:32 * h + 32], v, start=kt == 0, stop=kt == 8)
                if k1 == 9:
                    last.then_inc(s_pvs, 1)

            def combine(b, u):
                pe.wait_ge(s_os, b + 1)
                if not (isinstance(b, int) and b == 0):
                    pe.wait_ge(s_oct, b)
                mm(ps[:, 7, 256:288], osm[u], sel, start=True, stop=True).then_inc(s_cmb, 1)

            def sample(b, u, first=False, last=False):
                if not first:
                    combine(b - 1, 1 - u)
                if not last:
                    for g in range(4):
                        keys_transpose(b + 1, 1 - u, g)
                probs_transpose(b, u, 0)
                probs_transpose(b, u, 1)
                if not last:
                    keys_transpose(b + 1, 1 - u, 4)
                    keys_transpose(b + 1, 1 - u, 5)
                probs_transpose(b, u, 2)
                if not last:
                    keys_transpose(b + 1, 1 - u, 6)
                sample_values(b, u, 0, 5)
                if not last:
                    keys_transpose(b + 1, 1 - u, 7)
                sample_values(b, u, 5, 9)
                if not last:
                    sample_scores(b + 1)

            pe.wait_ge(s_dc, 2)
            for g in range(NPG):
                keys_transpose(0, 0, g, True)
            sample_scores(0)
            sample(0, 0, first=True)
            with pe.Fori(0, NB // 2 - 1) as jb:
                sample(2 * jb + 1, 1)
                sample(2 * jb + 2, 0)
            sample(NB - 1, 1, last=True)
            combine(NB - 1, 1)
            pe.wait_ge(s_lc, 5)
            pe.wait_ge(s_sq, 1)
            mm(ps[:, 6, 0:NB * 32], ones, oTq.rearrange("p b c -> p (b c)"), start=True, stop=True).then_inc(s_sqm, 1)

            pe.wait_ge(s_cat, 1)
            pe.wait_ge(s_wo, 16)

            def x1_transpose(t):
                pe.wait_ge(s_x1, t + 1)
                for half in range(2):
                    if t:
                        pe.wait_ge(s_x1e[half], t)
                    for kk in range(4):
                        k = 4 * half + kk
                        last = tr(ps[:, 4 + half, kk * P:kk * P + rows(t)], x[0:rows(t), t, k * P:(k + 1) * P], ident[0:rows(t), 0:rows(t)])
                    last.then_inc(s_x1t, 1)

            for t in range(NT):
                if t >= 2:
                    pe.wait_ge(s_opr, t - 1)
                for h in range(2):
                    for k in range(KD):
                        last = mm(ps[0:rows(t), 2 * (t % 2) + h, :], cat[:, k, t * P:t * P + rows(t)], wout[:, k, h * W:(h + 1) * W],
                                  start=k == 0, stop=k == KD - 1)
                last.then_inc(s_op, 1)
                if t:
                    x1_transpose(t - 1)
            x1_transpose(NT - 1)
            for h in range(2):
                pe.wait_ge(s_x1e[h], NT)
            pe.wait_ge(s_rt, 64)
            for h in range(2):
                for k in range(KD):
                    last = mm(ps[0:36, h, 0:HALF], wr[:, k, :], x1T[:, k, h * HALF:(h + 1) * HALF], start=k == 0, stop=k == KD - 1)
            last.then_inc(s_lg, 1)
            pe.wait_ge(s_lgc, 2)
            for t in range(NT):
                last = tr(ps[0:rows(t), 6, t * 36:t * 36 + 36], lgT[0:36, t * P:t * P + rows(t)], ident[0:36, 0:36])
            last.then_inc(s_lgt, 1)

            pe.wait_ge(s_oh, 1)
            mm(ps[:, 0, 0:NT * NE], tri, ohs.rearrange("p t e -> p (t e)"), start=True, stop=True)
            mm(ps[:, 1, 0:NT * NE], ones, ohs.rearrange("p t e -> p (t e)"), start=True, stop=True).then_inc(s_rk, 1)
            pe.wait_ge(s_ab, 1)
            for n in range(2 * NT):
                last = mm(ps[:, 2, 0:NPAIR], posoh[:, n, :], pairoh[:, n, :], start=n == 0, stop=n == 2 * NT - 1)
            last.then_inc(s_tab, 1)

            pe.wait_ge(s_info, 1)
            rounds = pe.value_load(info[0:1, 0:1], min_val=ROUND0, max_val=ROUNDS)

            def rows_transpose(j):
                pe.wait_ge(s_gx, 16 * j + 16)
                for half in range(2):
                    for kk in range(4):
                        k = 4 * half + kk
                        last = tr(ps[:, 2 + half, kk * P:(kk + 1) * P], xg.rearrange("p (c k) -> p k c", k=KD)[:, k, :], ident)
                    last.then_inc(s_xt, 1)

            rows_transpose(0)

            def pair(r, slot):
                j = RING * r + slot
                pe.wait_ge(s_xa, j + 1)
                pe.wait_ge(s_xd, j + 1)
                for u in range(2):
                    pe.wait_ge(s_wgu[slot][u], 32 * r + 32)
                    pe.wait_ge(s_info, 1)
                    gu = area(slot * 2 * TILEW + u * TILEW, 2, KD, FE)
                    for k in range(KD):
                        for fh in range(2):
                            last = mm(ps[fh * 64:fh * 64 + 64, u, 0:256], xTm[:, k, u * CAP:(u + 1) * CAP], gu[:, :, k, fh * P:(fh + 1) * P],
                                      start=k == 0, stop=k == KD - 1)
                    last.then_inc(s_gu[u], 1)

                def hidden_transpose(u):
                    pe.wait_ge(s_h[u], j + 1)
                    tr(ps[:, 4, u * P:(u + 1) * P], hid[u], ident).then_inc(s_ht[u], 1)

                def down(u):
                    pe.wait_ge(s_hc[u], j + 1)
                    pe.wait_ge(s_wd[slot][u], 16 * r + 16)
                    if not (isinstance(j, int) and j == 0):
                        pe.wait_ge(s_yc[u], j)
                    pe.wait_ge(s_info, 1)
                    dn = area(slot * 2 * TILEW + u * TILEW + GUW, 2, D)
                    for fh in range(2):
                        for dh in range(2):
                            last = mm(ps[dh * 64:dh * 64 + 64, 5 + u, :], hT[u][:, fh * CAP:(fh + 1) * CAP], dn[:, fh, dh * W:(dh + 1) * W],
                                      start=fh == 0, stop=fh == 1)
                    last.then_inc(s_y[u], 1)

                hidden_transpose(0)
                rows_transpose(j + 1)
                down(0)
                hidden_transpose(1)
                down(1)

            for slot in range(RING):
                pair(0, slot)
            with pe.Fori(1, rounds) as r:
                for slot in range(RING):
                    pair(r, slot)

        @block.scalar
        def _(act):
            a = nc.scalar
            act.wait_ge(s_zero, 1)
            for n in range(RING * ROUND0, RING * ROUNDS):
                act.dma_start(y_slots[n * P:(n + 1) * P, :], zeros).then_inc(s_fill, 16)
            act.dma_start(ptab[0:1, 0:NB * NPG], A["page_table"].rearrange("b n -> (b n)").unsqueeze(0)).then_inc(s_pt, 16)
            for n, name in enumerate(("lambda_q1", "lambda_k1", "lambda_q2", "lambda_k2")):
                act.dma_start(lamv[:, n, :], A[name][0:1, :].to_broadcast([P, BLK])).then_inc(s_ln1, 16)
            act.dma_start(g08, A["subln_g"][0].unsqueeze(1)).then_inc(s_ln1, 16)
            act.dma_start(lng, A["ln1_g"][0:1, :].to_broadcast([P, D])).then_inc(s_ln1, 16)
            act.dma_start(lnb, A["ln1_b"][0:1, :].to_broadcast([P, D])).then_inc(s_ln1, 16)

            def x_half(t, half, dst, src_sem, count, done):
                act.wait_ge(src_sem, count)
                a.copy(dst[:, 4 * half:4 * half + 4, t * P:t * P + rows(t)],
                       ps[:, 4 + half, :].rearrange("p (k c) -> p k c", k=4)[:, :, 0:rows(t)]).then_inc(done, 1)

            for t in range(NT):
                x_half(t, 1, xT, s_xtp, 2 * t + 2, s_xe[1])
            act.wait_ge(s_le, 1)
            a.activation(lex, lex, ACT.Exp).then_inc(s_lex, 1)
            unit = 4
            for m in range(4):
                act.wait_ge(s_pj, unit + m + 1)
                b = 2 * ((unit + m) % 2)
                for h in range(2):
                    a.activation(cat[:, 4 + m, h * HALF:(h + 1) * HALF], ps[:, b + h, 0:HALF], ACT.Gelu_apprx_tanh).then_inc(s_pev[(unit + m) % 2], 1)
            unit = 8
            act.wait_ge(s_prm, 1)
            for m in range(8):
                act.wait_ge(s_pj, unit + m + 1)
                b = 2 * ((unit + m) % 2)
                dst = (rg, ig)[m % 2]
                for h in range(2):
                    a.activation(dst[:, m // 2, h * HALF:(h + 1) * HALF], ps[:, b + h, 0:HALF], ACT.Sigmoid,
                                 bias=prm[:, m // 2, 5 + m % 2:6 + m % 2]).then_inc(s_pev[(unit + m) % 2], 1)
            unit = 16

            def q_unit(m):
                act.wait_ge(s_cst, 3)
                act.wait_ge(s_pj, unit + m + 1)
                b = 2 * ((unit + m) % 2)
                a.mul(qz[0:64, m, 0, 0:HALF], ps[0:64, b, 0:HALF], 0.125)
                a.mul(qz[0:64, m, 0, HALF:SEQ], ps[0:64, b + 1, 0:SEQ - HALF], 0.125)
                a.mul(qd[0:64, :, m, 0:SD], ps[0:64, b + 1, SEQ - HALF:HALF].rearrange("p (b s) -> p b s", s=SD), 0.125).then_inc(s_pev[(unit + m) % 2], 1)

            act.wait_ge(s_lam, 1)
            for n in range(2):
                act.wait_ge(s_pev[n], 16)
            for t in range(4):
                q_unit(t)
                a.activation(th[:, t, :], rg[:, t, :], ACT.Tanh, scale=cl[:, t, 0:1]).then_inc(s_th, 1)
                act.wait_ge(s_th, 2 * t + 1)
                a.activation(rg[:, t, :], rg[:, t, :], ACT.Exp, scale=cl[:, t, 0:1]).then_inc(s_th, 1)
            unit = 20
            for m in range(4):
                act.wait_ge(s_pj, unit + m + 1)
                b = 2 * ((unit + m) % 2)
                for h in range(2):
                    a.copy(kTn[:, m, h * HALF:(h + 1) * HALF], ps[:, b + h, 0:HALF]).then_inc(s_pev[(unit + m) % 2], 1)
                if m == 1:
                    act.wait_ge(s_m2, 1)
                    a.activation(th, th, ACT.Sqrt).then_inc(s_mult, 1)
            unit = 24
            for t in range(NT):
                act.wait_ge(s_cst, 3)
                act.wait_ge(s_pj, unit + t + 1)
                b = 2 * ((unit + t) % 2)
                a.copy(vn[0:rows(t), t, :], ps[0:rows(t), b, :]).then_inc(s_pev[(unit + t) % 2], 2)
            act.wait_ge(s_dc, 1)
            a.activation(sc[:, 4:6], sc[:, 0:2], ACT.Exp).then_inc(s_lexp, 1)

            for t in range(NT):
                act.wait_ge(s_kt, t + 1)
                if t >= 2:
                    act.wait_ge(s_kout[t % 2], 16 * (t // 2))
                a.copy(kstage[0:rows(t), t % 2, :], ps[0:rows(t), 4 + t % 2, :]).then_inc(s_kc, 1)
            act.wait_ge(s_endp, 1)
            a.copy(ends_out[0:36, :], ps[0:36, 6, :]).then_inc(s_endc, 1)

            steps = [(i, h) for i in range(NT - 1) for h in range(NH)]

            def exps(n):
                i, h = steps[n]
                act.wait_ge(s_mxp, n + 1)
                if n >= 2:
                    act.wait_ge(s_w, n - 1)
                for m in range(2):
                    last = a.activation(pexp[n % 2][:, m, 0:(i + 1) * P], ps[:, 2 * (n % 2) + m, 0:(i + 1) * P], ACT.Exp,
                                        bias=mx[:, n % 2, m:m + 1], accum_out=sm[:, n % 2, m:m + 1])
                last.then_inc(s_exp, 1)

            def o_out(i):
                act.wait_ge(s_ot, i + 1)
                a.activation(cat[:, 0:NH, i * P:(i + 1) * P], ps[:, 7, :].rearrange("p (h c) -> p h c", h=NH), ACT.Copy,
                             scale=g08[:, 0:1]).then_inc(s_oe, 1)

            def weights_out(n):
                i, h = steps[n]
                act.wait_ge(s_wt, n + 1)
                if n >= 2:
                    act.wait_ge(s_pvp, n - 1)
                a.copy(wT[n % 2][:, 0:(i + 1) * P], ps[:, 4 + n % 2, 0:(i + 1) * P]).then_inc(s_wc, 1)

            exps(0)
            exps(1)
            weights_out(0)
            exps(2)
            for n, (i, h) in enumerate(steps):
                if n + 1 < len(steps):
                    weights_out(n + 1)
                if h == NH - 1:
                    act.wait_ge(s_pvp, n + 1)
                    if i:
                        act.wait_ge(s_ot, i)
                    a.copy(osb.rearrange("p h c -> p (h c)"), ps[:, 6, :]).then_inc(s_oc, 1)
                if n + 3 < len(steps):
                    exps(n + 3)
                if h == 2 and i:
                    o_out(i - 1)
            o_out(NT - 2)

            act.wait_ge(s_sp, len(steps))
            act.dma_start(wr[:, :, 0:NG], A["w_group_router"][0].rearrange("(k p) g -> p k g", p=P)).then_inc(s_rt, 16)
            act.dma_start(wr[:, :, NG:NG + NE], A["w_expert_router"][0].rearrange("(k p) g -> p k g", p=P)).then_inc(s_rt, 16)
            act.dma_start(rbias[:, 0:NG], A["b_group_router"][0:1, :].to_broadcast([P, NG])).then_inc(s_rt, 16)
            act.dma_start(rbias[:, NG:NG + NE], A["b_expert_router"][0:1, :].to_broadcast([P, NE])).then_inc(s_rt, 16)

            def probs(b, grp):
                act.wait_ge(s_ptp, 3 * b + grp + 1)
                act.wait_ge(s_cst, 3)
                k0, k1 = ((0, 4), None, (8, 9))[grp]
                a.copy(pT[:, k0:k1, :], ps[:, 5, 0:(k1 - k0) * P].rearrange("p (k c) -> p k c", c=P)).then_inc(s_pta, 1)

            def keys_out(b, g):
                act.wait_ge(s_ktp[0], 4 * b + g // 2 + 1)
                act.wait_ge(s_sc, b)
                a.copy(kT[:, :, g * P:(g + 1) * P], ps[:, 3, :].rearrange("p (h c) -> p h c", h=NH)).then_inc(s_ktc[0], 1)

            def sample(b, u, last=False):
                if not last:
                    keys_out(b + 1, 0)
                act.wait_ge(s_mxs, b + 1)
                act.wait_ge(s_cst, 3)
                a.activation(pes[u].rearrange("p (c k) j -> p c (k j)", c=3), ps[:, 0:3, 0:384], ACT.Exp,
                             bias=coef[:, u:u + 1], accum_out=coef[:, 2 + u:3 + u]).then_inc(s_exs, 1)
                if not last:
                    keys_out(b + 1, 2)
                probs(b, 0)
                if not last:
                    keys_out(b + 1, 4)
                probs(b, 2)
                if not last:
                    keys_out(b + 1, 6)

            for g in range(0, NPG, 2):
                keys_out(0, g)
            sample(0, 0)
            with act.Fori(0, NB // 2 - 1) as jb:
                sample(2 * jb + 1, 1)
                sample(2 * jb + 2, 0)
            sample(NB - 1, 1, last=True)
            act.wait_ge(s_sq, 2)
            a.activation(oTr, oTr, ACT.Sqrt).then_inc(s_srs, 1)

            def x1_half(t):
                x_half(t, 1, x1T, s_x1t, 2 * t + 2, s_x1e[1])

            for t in range(NT):
                r = rows(t)
                act.wait_ge(s_rstd, t + 1)
                act.wait_ge(s_mvn, t + 1)
                a.activation(x[0:r, t, :], x[0:r, t, :], ACT.Identity, scale=pw[0:r, t:t + 1], bias=mv[0:r, t, 0:1]).then_inc(s_nrm, 1)
                if t:
                    x1_half(t - 1)
                    act.wait_ge(s_x1, t)
                    act.dma_start(x1_dram[(t - 1) * P:t * P, :], x[:, t - 1, :]).then_inc(s_x1d, 16)
            act.wait_ge(s_x1, NT)
            act.dma_start(x1_dram[SEQ:T, :], x[0:TS, NT - 1, :]).then_inc(s_x1d, 16)
            x1_half(NT - 1)
            act.dma_start(lng, A["ln2_g"][0:1, :].to_broadcast([P, D])).then_inc(s_ln2, 16)
            act.dma_start(lnb, A["ln2_b"][0:1, :].to_broadcast([P, D])).then_inc(s_ln2, 16)
            act.wait_ge(s_lg, 1)
            for h in range(2):
                last = a.copy(lgT[0:36, h * HALF:(h + 1) * HALF], ps[0:36, h, 0:HALF])
                last.then_inc(s_lgc, 1)
            act.wait_ge(s_re, 1)
            a.activation(rexp, rexp, ACT.Exp).then_inc(s_rx, 1)

            act.wait_ge(s_info, 1)
            rounds = act.value_load(info[0:1, 0:1], min_val=ROUND0, max_val=ROUNDS)

            def x_rows(j):
                act.wait_ge(s_xt, 2 * j + 1)
                act.wait_ge(s_info, 1)
                a.copy(xTm[:, 0:4, :].rearrange("p k c -> p (k c)"), ps[:, 2, :]).then_inc(s_xa, 1)

            x_rows(0)

            def pair(r, slot):
                j = RING * r + slot
                for u in range(2):
                    act.wait_ge(s_gu[u], j + 1)
                    a.activation(sg[u], ps[:, u, 0:P], ACT.Silu).then_inc(s_sg[u], 1)
                x_rows(j + 1)
                for u in range(2):
                    act.wait_ge(s_y[u], j + 1)
                    if not (isinstance(j, int) and j == 0):
                        act.wait_ge(s_yd[u], 32 * j)
                    a.copy(ysb[u], ps[:, 5 + u, :]).then_inc(s_yc[u], 1)
                    act.wait_ge(s_yc[u], j + 1)
                    for dh in range(2):
                        act.dma_start(y_slots[bass.ds((2 * j + u) * CAP, CAP), dh * W:(dh + 1) * W], ysb[u][dh * 64:dh * 64 + 64, :]).then_inc(s_yd[u], 16)

            for slot in range(RING):
                pair(0, slot)
            with act.Fori(1, rounds) as r:
                for slot in range(RING):
                    pair(r, slot)

            for t in range(NT):
                r = rows(t)
                act.wait_ge(s_rstd2, t + 1)
                act.wait_ge(s_mvn, NT + t + 1)
                a.activation(x[0:r, t, :], x[0:r, t, :], ACT.Identity, scale=pw[0:r, t:t + 1], bias=mv[0:r, t, 0:1]).then_inc(s_nrm2, 1)

        @block.vector
        def _(dve):
            v = nc.vector
            cnt = [0]

            def link(ins):
                cnt[0] += 1
                ins.then_inc(s_ch, 1)
                dve.wait_ge(s_ch, cnt[0])

            def x_half(t, dst, src_sem, count, done):
                dve.wait_ge(src_sem, count)
                v.tensor_copy(dst[:, 0:4, t * P:t * P + rows(t)],
                              ps[:, 4, :].rearrange("p (k c) -> p k c", k=4)[:, :, 0:rows(t)]).then_inc(done, 1)

            for t in range(NT):
                x_half(t, xT, s_xtp, 2 * t + 1, s_xe[0])
            dve.wait_ge(s_rows, 1)
            v.tensor_copy(prm, ps[:, 6, 0:160].rearrange("p (t c) -> p t c", c=40)).then_inc(s_prm, 1)
            dve.wait_ge(s_prm, 1)
            dve.wait_ge(s_cst, 3)
            link(v.tensor_copy(xl[:, :, XSEG:].rearrange("p t (b c) -> p t b c", c=SSEG)[:, :, :, 0:3],
                               prm[:, :, 16:40].rearrange("p t (b j) -> p t b j", j=3)))
            y, e = cl[:, :, 0:1], cl[:, :, 1:2]
            s, s2 = cl[:, :, 2:3], cl[:, :, 3:4]
            link(v.tensor_scalar(y, prm[:, :, 7:8], -1.0, None, ALU.mult))
            link(v.tensor_tensor(e, y, prm[:, :, 7:8], ALU.min))
            v.tensor_copy(lex, e).then_inc(s_le, 1)
            for m in range(4):
                dve.wait_ge(s_pj, m + 1)
                b = 2 * (m % 2)
                v.tensor_copy(xl[:, m, 3:3 + HALF], ps[:, b, 0:HALF])
                v.tensor_copy(xl[:, m, 3 + HALF:XSEG], ps[:, b + 1, 0:SEQ - HALF]).then_inc(s_pev[m % 2], 1)
                v.tensor_copy(xl[:, m, XSEG:].rearrange("p (b c) -> p b c", c=SSEG)[:, :, 3:],
                              ps[:, b + 1, SEQ - HALF:HALF].rearrange("p (b s) -> p b s", s=SD)).then_inc(s_pev[m % 2], 1)
                dve.wait_ge(s_pev[m % 2], 2 * (m // 2) + 2)
                xs = xl[:, m, XSEG:].rearrange("p (b c) -> p b c", c=SSEG)
                op, osmp = xc[:, m, 0:SEQ], xc[:, m, SEQ:T].rearrange("p (b s) -> p b s", s=SD)
                v.tensor_scalar(op, xl[:, m, 0:SEQ], prm[:, m, 0:1], prm[:, m, 4:5], ALU.mult, ALU.add)
                link(v.tensor_scalar(osmp, xs[:, :, 0:SD], prm[:, m, 0:1], prm[:, m, 4:5], ALU.mult, ALU.add))
                for j in range(1, 4):
                    v.scalar_tensor_tensor(out=op, in0=xl[:, m, j:j + SEQ], scalar=prm[:, m, j:j + 1], in1=op, op0=ALU.mult, op1=ALU.add)
                    last = v.scalar_tensor_tensor(out=osmp, in0=xs[:, :, j:j + SD], scalar=prm[:, m, j:j + 1], in1=osmp, op0=ALU.mult, op1=ALU.add)
                    link(last)
                dve.sem_inc(s_xc, 1)
            dve.wait_ge(s_lex, 1)
            link(v.tensor_scalar(s2, lex, 2.0, None, ALU.add))
            link(v.reciprocal(s2, s2))
            link(v.tensor_tensor(s, lex, s2, ALU.mult))
            link(v.tensor_tensor(s2, s, s, ALU.mult))
            link(v.tensor_scalar(e, s2, 1.0 / 15, 1.0 / 13, ALU.mult, ALU.add))
            for n in (11, 9, 7, 5, 3, 1):
                link(v.tensor_tensor(e, e, s2, ALU.mult))
                link(v.tensor_scalar(e, e, 1.0 / n, None, ALU.add))
            link(v.tensor_tensor(e, e, s, ALU.mult))
            link(v.tensor_scalar(y, y, 0.0, -LRU_C, ALU.max, ALU.mult))
            link(v.scalar_tensor_tensor(out=y, in0=e, scalar=-2.0 * LRU_C, in1=y, op0=ALU.mult, op1=ALU.add))
            dve.sem_inc(s_lam, 1)

            dve.wait_ge(s_ln1, 16 * 7)
            link(v.tensor_tensor(lamv[:, 0, :], lamv[:, 0, :], lamv[:, 1, :], ALU.mult))
            link(v.tensor_tensor(lamv[:, 2, :], lamv[:, 2, :], lamv[:, 3, :], ALU.mult))
            link(v.tensor_reduce(sc[:, 0:1], lamv[:, 0, :], AX.X, ALU.add))
            link(v.tensor_reduce(sc[:, 1:2], lamv[:, 2, :], AX.X, ALU.add))
            link(v.tensor_scalar(g08, g08, 1.0 - LAM_INIT, None, ALU.mult))
            sel0, sel1 = sel01
            link(v.tensor_copy(iotf, ioti))
            link(v.tensor_scalar(parti, parti, SD - 1, None, ALU.bitwise_and))
            link(v.tensor_copy(partf, parti))
            link(v.tensor_scalar(bigm, iotf, partf[:, 0:1], None, ALU.is_le))
            link(v.scalar_tensor_tensor(out=bigm, in0=iotf, scalar=0.0, in1=bigm, op0=ALU.is_ge, op1=ALU.mult))
            link(v.tensor_scalar(bigm, bigm, 1.0, -NEG, ALU.subtract, ALU.mult))
            link(v.tensor_tensor(sel, sel0, sel1, ALU.add))
            link(v.tensor_reduce(sc[:, 6:7], sel0, AX.X, ALU.add))
            link(v.tensor_reduce(sc[:, 7:8], sel1, AX.X, ALU.add))
            dve.sem_inc(s_dc, 1)

            unit = 16
            for m in range(4):
                dve.wait_ge(s_pj, unit + m + 1)
                b = 2 * ((unit + m) % 2)
                v.tensor_scalar(qz[64:P, m, 1, 0:HALF], ps[64:P, b, 0:HALF], 0.125, None, ALU.mult)
                v.tensor_scalar(qz[64:P, m, 1, HALF:SEQ], ps[64:P, b + 1, 0:SEQ - HALF], 0.125, None, ALU.mult)
                v.tensor_scalar(qd[64:P, :, m, SD:2 * SD], ps[64:P, b + 1, SEQ - HALF:HALF].rearrange("p (b s) -> p b s", s=SD),
                                0.125, None, ALU.mult).then_inc(s_pev[(unit + m) % 2], 1)
            dve.wait_ge(s_th, 8)
            dve.wait_ge(s_fill, 16 * RING * (ROUNDS - ROUND0))
            link(v.tensor_scalar(hh, th, -1.0, 1.0, ALU.mult, ALU.add))
            link(v.reciprocal(hh, hh))
            link(v.scalar_tensor_tensor(out=th, in0=th, scalar=-2.0, in1=hh, op0=ALU.mult, op1=ALU.mult))
            link(v.tensor_scalar(th, th, 0.0, None, ALU.max))
            dve.sem_inc(s_m2, 1)
            link(v.tensor_tensor(ig, ig, xc, ALU.mult))
            dve.wait_ge(s_mult, 1)
            link(v.tensor_tensor(ig, ig, th, ALU.mult))
            a0 = rg[:, :, SEQ:T].rearrange("p t (b s) -> p t b s", s=SD)[:, :, :, 0]
            u0 = ig[:, :, SEQ:T].rearrange("p t (b s) -> p t b s", s=SD)[:, :, :, 0]
            link(v.tensor_tensor(th[:, :, 0:NB], a0, prm[:, :, 8:16], ALU.mult))
            link(v.tensor_tensor(u0, u0, th[:, :, 0:NB], ALU.add))
            link(v.tensor_scalar(a0, a0, 0.0, None, ALU.mult))
            for t in range(4):
                link(v.tensor_tensor_scan(hh[:, t, :], rg[:, t, :], ig[:, t, :], 0.0, ALU.mult, ALU.add))
            link(v.tensor_tensor(cat[:, 4:8, :], cat[:, 4:8, :], hh, ALU.mult))
            v.tensor_copy(ends[:, :, 0:1], hh[:, :, SEQ - 1:SEQ])
            v.tensor_copy(ends[:, :, 1:9], hh[:, :, SEQ:T].rearrange("p t (b s) -> p t b s", s=SD)[:, :, :, SD - 1])
            v.tensor_copy(ends[:, :, 9:12], xl[:, :, XSEG - 3:XSEG])
            link(v.tensor_copy(ends[:, :, 12:36].rearrange("p t (b j) -> p t b j", j=3),
                               xl[:, :, XSEG:].rearrange("p t (b c) -> p t b c", c=SSEG)[:, :, :, SD:SSEG]))
            dve.sem_inc(s_ends, 1)
            dve.wait_ge(s_lexp, 1)
            link(v.tensor_tensor(sc[:, 8:9], sc[:, 5:6], sc[:, 4:5], ALU.subtract))
            link(v.tensor_scalar(sc[:, 8:9], sc[:, 8:9], -LAM_INIT, None, ALU.add))
            link(v.scalar_tensor_tensor(out=sc[:, 9:10], in0=sc[:, 7:8], scalar=sc[:, 8:9], in1=sc[:, 6:7], op0=ALU.mult, op1=ALU.add))

            steps = [(i, h) for i in range(NT - 1) for h in range(NH)]

            def maxima(n):
                i, h = steps[n]
                dve.wait_ge(s_sp, n + 1)
                sps = ps[:, 2 * (n % 2):2 * (n % 2) + 2, 0:(i + 1) * P]
                link(v.tensor_tensor(sps[:, :, i * P:], sps[:, :, i * P:], dmask.unsqueeze(1).broadcast_to([P, 2, P]), ALU.add))
                link(v.tensor_reduce(mx[:, n % 2, :], sps, AX.X, ALU.max, negate=True))
                dve.sem_inc(s_mxp, 1)

            def weights_(n):
                i, h = steps[n]
                dve.wait_ge(s_exp, n + 1)
                if n >= 2:
                    dve.wait_ge(s_wt, n - 1)
                link(v.reciprocal(rc[:, n % 2, :], sm[:, n % 2, :]))
                link(v.tensor_scalar(rc[:, n % 2, 1:2], rc[:, n % 2, 1:2], sc[:, 8:9], None, ALU.mult))
                wd_, pe_ = wdiff[n % 2][:, 0:(i + 1) * P], pexp[n % 2]
                link(v.tensor_scalar(wd_, pe_[:, 0, 0:(i + 1) * P], rc[:, n % 2, 0:1], None, ALU.mult))
                v.scalar_tensor_tensor(out=wd_, in0=pe_[:, 1, 0:(i + 1) * P], scalar=rc[:, n % 2, 1:2], in1=wd_, op0=ALU.mult, op1=ALU.add).then_inc(s_w, 1)

            def squares(i):
                if i == 0:
                    dve.wait_ge(s_out, 16 * 6)
                dve.wait_ge(s_oc, i + 1)
                link(v.tensor_tensor(osq, osb, osb, ALU.mult))
                link(v.tensor_reduce(ss, osq, AX.X, ALU.add))
                v.tensor_scalar(ss, ss, 1.0 / P, EPS, ALU.mult, ALU.add).then_inc(s_var, 1)

            def norm(i):
                dve.wait_ge(s_rs, i + 1)
                v.tensor_tensor(osb, osb, ss.unsqueeze(2).broadcast_to([P, NH, P]), ALU.mult).then_inc(s_on, 1)

            maxima(0)
            maxima(1)
            weights_(0)
            weights_(1)
            maxima(2)
            for n, (i, h) in enumerate(steps):
                if n + 2 < len(steps):
                    weights_(n + 2)
                if n + 3 < len(steps):
                    maxima(n + 3)
                if i and h == 0:
                    squares(i - 1)
                if i and h == 1:
                    norm(i - 1)
            squares(NT - 2)
            norm(NT - 2)

            dve.wait_ge(s_sp, len(steps))
            link(v.tensor_copy(kT[:, :, PAST:PAST + TS], kTn[:, :, SEQ:T]))
            link(v.memset(kT[:, :, PAST + TS:], 0.0))
            dve.sem_inc(s_dc, 1)
            step = [0]
            PER = 2

            def chain(b, ins):
                step[0] += 1
                ins.then_inc(s_sch, 1)
                dve.wait_ge(s_sch, PER * b + (step[0] - 1) % PER + 1)

            def keys_out(b, g):
                dve.wait_ge(s_ktp[1], 4 * b + g // 2 + 1)
                dve.wait_ge(s_sc, b)
                v.tensor_copy(kT[:, :, g * P:(g + 1) * P], ps[:, 4, :].rearrange("p (h c) -> p h c", h=NH)).then_inc(s_ktc[1], 1)

            def combined_out(b):
                dve.wait_ge(s_cmb, b + 1)
                dve.wait_ge(s_cst, 3)
                v.tensor_copy(arena[:, bass.ds(A_STG + W + 32 * b, 32)], ps[:, 7, 256:288]).then_inc(s_oct, 1)

            def sample(b, u, first=False, last=False):
                dve.wait_ge(s_sc, b + 1)
                dve.wait_ge(s_cst, 3)
                new = ps[:, 2, 256:384]
                v.tensor_tensor(new, new, bigm[:, bass.ds(56 - 8 * b, P)], ALU.add).then_inc(s_msk, 1)
                dve.wait_ge(s_msk, b + 1)
                dve.wait_ge(s_cst, 3)
                v.tensor_reduce(coef[:, u:u + 1], ps[:, 0:3, 0:384], AX.XY, ALU.max, negate=True).then_inc(s_mxs, 1)
                if not last:
                    keys_out(b + 1, 1)
                if not first:
                    combined_out(b - 1)
                if not last:
                    keys_out(b + 1, 3)
                dve.wait_ge(s_ptp, 3 * b + 2)
                dve.wait_ge(s_cst, 3)
                v.tensor_copy(pT[:, 4:8, :], ps[:, 6, :].rearrange("p (k c) -> p k c", c=P)).then_inc(s_ptd, 1)
                if not last:
                    keys_out(b + 1, 5)
                dve.wait_ge(s_exs, b + 1)
                chain(b, v.reciprocal(sc[:, 10 + u:11 + u], coef[:, 2 + u:3 + u]))
                chain(b, v.tensor_tensor(sc[:, 10 + u:11 + u], sc[:, 10 + u:11 + u], sc[:, 9:10], ALU.mult))
                if not last:
                    keys_out(b + 1, 7)
                dve.wait_ge(s_pvs, b + 1)
                dve.wait_ge(s_cst, 3)
                v.tensor_scalar(osm[u], ps[:, 7, 0:P], sc[:, 10 + u:11 + u], None, ALU.mult).then_inc(s_os, 1)

            for g in range(1, NPG, 2):
                keys_out(0, g)
            sample(0, 0, first=True)
            with dve.Fori(0, NB // 2 - 1) as jb:
                sample(2 * jb + 1, 1)
                sample(2 * jb + 2, 0)
            sample(NB - 1, 1, last=True)
            combined_out(NB - 1)
            dve.wait_ge(s_oct, NB)
            v.tensor_tensor(oTq, oTs, oTs, ALU.mult).then_inc(s_sq, 1)
            dve.wait_ge(s_sqm, 1)
            link(v.tensor_scalar(oTr.rearrange("p b c -> p (b c)"), ps[:, 6, 0:NB * 32], 1.0 / P, EPS, ALU.mult, ALU.add))
            v.reciprocal(oTr, oTr).then_inc(s_sq, 1)
            dve.wait_ge(s_srs, 1)
            link(v.tensor_tensor(oTs, oTs, oTr, ALU.mult))
            dve.wait_ge(s_oe, NT - 1)
            link(v.tensor_scalar(cat[:, 0:NH, SEQ:T].rearrange("p h (b s) -> p b h s", s=SD),
                                 oTs.rearrange("p b (h s) -> p b h s", s=SD), g08[:, 0:1], None, ALU.mult))
            dve.sem_inc(s_cat, 1)

            def stats(t, done):
                r = rows(t)
                v.bn_stats(st[0:r, 0:6], x[0:r, t, 0:512])
                link(v.bn_stats(st[0:r, 6:12], x[0:r, t, 512:D]))
                link(v.bn_aggr(mv[0:r, t, :], st[0:r, :]))
                v.tensor_scalar(pw[0:r, t:t + 1], mv[0:r, t, 1:2], EPS, None, ALU.add).then_inc(done, 1)

            def neg_mean(t, ready, n):
                r = rows(t)
                dve.wait_ge(ready, n)
                v.scalar_tensor_tensor(out=mv[0:r, t, 0:1], in0=mv[0:r, t, 0:1], scalar=-1.0, in1=pw[0:r, t:t + 1], op0=ALU.mult, op1=ALU.mult).then_inc(s_mvn, 1)

            def gain(t):
                r = rows(t)
                dve.wait_ge(s_nrm, t + 1)
                link(v.tensor_tensor(x[0:r, t, :], x[0:r, t, :], lng[0:r, :], ALU.mult))
                v.tensor_tensor(x[0:r, t, :], x[0:r, t, :], lnb[0:r, :], ALU.add).then_inc(s_x1, 1)

            link(v.memset(pw, 1.0))
            for t in range(NT):
                r = rows(t)
                dve.wait_ge(s_op, t + 1)
                link(v.scalar_tensor_tensor(out=x[0:r, t, :], in0=x[0:r, t, :], scalar=ALPHA,
                                            in1=ps[0:r, 2 * (t % 2):2 * (t % 2) + 2, :].rearrange("p a b -> p (a b)"), op0=ALU.mult, op1=ALU.add))
                dve.sem_inc(s_opr, 1)
                stats(t, s_mv)
                neg_mean(t, s_rstd, t + 1)
                gain(t)
                if t:
                    x_half(t - 1, x1T, s_x1t, 2 * (t - 1) + 1, s_x1e[0])
            x_half(NT - 1, x1T, s_x1t, 2 * NT - 1, s_x1e[0])

            link(v.memset(L, 0.0))
            dve.wait_ge(s_lgt, 1)
            psl = ps[:, 6, 0:NT * 36].rearrange("p (t c) -> p t c", c=36)
            v.tensor_tensor(L[:, 0:NT - 1, :], psl[:, 0:NT - 1, :], rbias.unsqueeze(1).broadcast_to([P, NT - 1, 36]), ALU.add)
            link(v.tensor_tensor(L[0:TS, NT - 1, :], psl[0:TS, NT - 1, :], rbias[0:TS, :], ALU.add))
            dve.wait_ge(s_lc, 5)
            link(v.tensor_copy(io128f, io128i))
            link(v.tensor_copy(tokf, toki))
            link(v.tensor_scalar(valid, tokf, float(T), None, ALU.is_lt))
            link(v.tensor_scalar(capt, io128f[:, 0:MOREQ], 1.0, float(CAP), ALU.add, ALU.mult))
            link(v.tensor_scalar(pairt, io128f[:, 0:NPAIR - 1], 1.0, float(P), ALU.add, ALU.mult))

            def over(ap, m):
                return ap.unsqueeze(2).broadcast_to([P, ap.shape[1], m])

            def under(ap, n):
                return ap.unsqueeze(1).broadcast_to([P, n, ap.shape[1]])

            def first_max(src, n, out_max, onehot, tmp):
                link(v.tensor_reduce(out_max, src, AX.X, ALU.max))
                link(v.tensor_tensor(tmp, src, over(out_max, n), ALU.is_equal))
                link(v.tensor_scalar(tmp, tmp, -1000.0, None, ALU.mult))
                link(v.tensor_tensor(tmp, tmp, under(io128f[:, 0:n], NT), ALU.add))
                link(v.tensor_reduce(first, tmp, AX.X, ALU.min))
                link(v.tensor_tensor(onehot, tmp, over(first, n), ALU.is_equal))

            first_max(L[:, :, 0:NG], NG, gmax, goh, t8[:, :, 0:NG])
            link(v.tensor_tensor(rexp[:, :, 0:NG], L[:, :, 0:NG], over(gmax, NG), ALU.subtract))
            el = L[:, :, NG:].rearrange("p t (g e) -> p t g e", g=NG)
            ing = ohs.rearrange("p t (g e) -> p t g e", g=NG)
            link(v.tensor_tensor(ing, el, goh.unsqueeze(3).broadcast_to([P, NT, NG, EPG]), ALU.mult))
            link(v.tensor_reduce(wi, ohs.rearrange("p t (g e) -> p t e g", g=NG), AX.X, ALU.add))
            first_max(wi, EPG, m1, oh1, t8)
            link(v.scalar_tensor_tensor(out=wi, in0=oh1, scalar=-3e38, in1=wi, op0=ALU.mult, op1=ALU.add))
            first_max(wi, EPG, m2, oh2, t8)
            link(v.tensor_tensor(rexp[:, :, NG], m2, m1, ALU.subtract))
            dve.sem_inc(s_re, 1)
            link(v.tensor_tensor(goh, goh, over(valid, NG), ALU.mult))
            for k, oh in enumerate((oh1, oh2)):
                link(v.tensor_tensor(ek[:, k * NT:(k + 1) * NT, :].rearrange("p t (g e) -> p t g e", g=NG),
                                     goh.unsqueeze(3).broadcast_to([P, NT, NG, EPG]),
                                     oh.unsqueeze(2).broadcast_to([P, NT, NG, EPG]), ALU.mult))
            link(v.tensor_tensor(ohs, ek[:, 0:NT, :], ek[:, NT:, :], ALU.add))
            dve.sem_inc(s_oh, 1)
            dve.wait_ge(s_rx, 1)
            link(v.tensor_reduce(m1, rexp[:, :, 0:NG], AX.X, ALU.add))
            link(v.tensor_scalar(m2, rexp[:, :, NG], 1.0, None, ALU.add))
            link(v.tensor_tensor(m1, m1, m2, ALU.mult))
            link(v.reciprocal(wgt[:, 0, :], m1))
            link(v.tensor_tensor(wgt[:, 1, :], wgt[:, 0, :], rexp[:, :, NG], ALU.mult))
            dve.wait_ge(s_rk, 1)
            tot = ps[:, 1, 0:NT * NE].rearrange("p (t e) -> p t e", e=NE)
            link(v.tensor_copy(rank, ps[:, 0, 0:NT * NE].rearrange("p (t e) -> p t e", e=NE)))
            link(v.tensor_copy(run, tot[:, 0, :]))
            for t in range(1, NT):
                link(v.tensor_tensor(rank[:, t, :], rank[:, t, :], run, ALU.add))
                link(v.tensor_tensor(run, run, tot[:, t, :], ALU.add))
            full = cmp8.rearrange("p a b -> p (a b)")[:, 0:NE * MOREQ].rearrange("p (e n) -> p e n", n=MOREQ)
            link(v.tensor_tensor(full, over(run, MOREQ), under(capt, NE), ALU.is_gt))
            link(v.tensor_reduce(more, full, AX.X, ALU.add))
            link(v.tensor_scalar(run, run, 0.0, 1.0, ALU.mult, ALU.add))
            link(v.tensor_tensor_scan(upto, run, more, 0.0, ALU.mult, ALU.add))
            link(v.tensor_tensor(before, upto, more, ALU.subtract))
            tables = (rk, rank.unsqueeze(1).broadcast_to([P, 2, NT, NE])), \
                (rb, before.unsqueeze(1).unsqueeze(1).broadcast_to([P, 2, NT, NE])), \
                (re_, io128f[:, 0:NE].unsqueeze(1).unsqueeze(1).broadcast_to([P, 2, NT, NE]))
            for dst, table in tables:
                link(v.tensor_tensor(ekx.rearrange("p (k t) e -> p k t e", k=2), ek.rearrange("p (k t) e -> p k t e", k=2), table, ALU.mult))
                link(v.tensor_reduce(dst, ekx, AX.X, ALU.add))
            link(v.tensor_tensor(cmp8[:, :, 0:MOREQ], over(rk, MOREQ), under(capt, 2 * NT), ALU.is_ge))
            link(v.tensor_reduce(rf, cmp8[:, :, 0:MOREQ], AX.X, ALU.add))
            link(v.tensor_tensor(rb, rb, rf, ALU.add))
            link(v.scalar_tensor_tensor(out=rb, in0=rb, scalar=float(NE - 1), in1=re_, op0=ALU.add, op1=ALU.subtract))
            link(v.scalar_tensor_tensor(out=rb, in0=rf, scalar=1.0, in1=rb, op0=ALU.is_ge, op1=ALU.mult))
            link(v.tensor_tensor(rb, rb, re_, ALU.add))
            link(v.tensor_tensor(rb, rb, rf, ALU.subtract))
            link(v.scalar_tensor_tensor(out=rs, in0=rb, scalar=float(CAP), in1=rk, op0=ALU.mult, op1=ALU.add))
            link(v.tensor_tensor(cmp8[:, :, 0:NPAIR - 1], over(rs, NPAIR - 1), under(pairt, 2 * NT), ALU.is_ge))
            link(v.tensor_reduce(rf, cmp8[:, :, 0:NPAIR - 1], AX.X, ALU.add))
            link(v.scalar_tensor_tensor(out=rb, in0=rf, scalar=-float(P), in1=rs, op0=ALU.mult, op1=ALU.add))
            link(v.tensor_tensor(posoh, under(io128f, 2 * NT), over(rb, P), ALU.is_equal))
            link(v.tensor_tensor(pairoh, under(io128f[:, 0:NPAIR], 2 * NT), over(rf, NPAIR), ALU.is_equal))
            link(v.tensor_tensor(tokf, tokf, valid, ALU.mult))
            for k in range(2):
                link(v.tensor_tensor(pairoh[:, k * NT:(k + 1) * NT, :], pairoh[:, k * NT:(k + 1) * NT, :], over(tokf, NPAIR), ALU.mult))
            dve.sem_inc(s_ab, 1)
            link(v.tensor_copy(yidx.rearrange("p k t -> p (k t)"), rs))
            link(v.tensor_scalar(one[:, 0:1], upto[:, NE - 1:NE], 4.0, float(ROUND0), ALU.is_gt, ALU.add))
            for n in (10.0, 16.0):
                link(v.scalar_tensor_tensor(out=one[:, 0:1], in0=upto[:, NE - 1:NE], scalar=n, in1=one[:, 0:1], op0=ALU.is_gt, op1=ALU.add))
            link(v.tensor_copy(info[:, 0:1], one[:, 0:1]))
            link(v.tensor_copy(info[:, 1:3], io128f[:, TAB0:TAB0 + 2]))
            link(v.tensor_tensor(xsel, under(before, NEXTRA), over(io128f[:, 0:NEXTRA], NE), ALU.is_le))
            link(v.tensor_tensor(xsel2, under(upto, NEXTRA), over(io128f[:, 0:NEXTRA], NE), ALU.is_gt))
            link(v.tensor_tensor(xsel, xsel, xsel2, ALU.mult))
            link(v.tensor_tensor(xsel, xsel, under(io128f[:, 0:NE], NEXTRA), ALU.mult))
            link(v.tensor_reduce(xsel2[:, 0, 0:NEXTRA], xsel, AX.X, ALU.add))
            link(v.tensor_copy(info[:, 3:NEXTRA + 3], xsel2[:, 0, 0:NEXTRA]))
            dve.wait_ge(s_tab, 1)
            link(v.tensor_copy(idx, ps[:, 2, 0:NPAIR]))
            dve.sem_inc(s_info, 1)

            rounds = dve.value_load(info[0:1, 0:1], min_val=ROUND0, max_val=ROUNDS)
            pairs = dve.snap(rounds * RING)

            def x_rows(j):
                dve.wait_ge(s_xt, 2 * j + 2)
                dve.wait_ge(s_info, 1)
                v.tensor_copy(xTm[:, 4:8, :].rearrange("p k c -> p (k c)"), ps[:, 3, :]).then_inc(s_xd, 1)

            dve.wait_ge(s_x1d, 16 * NT)
            for t in range(NT):
                v.tensor_scalar(x[0:rows(t), t, :], x[0:rows(t), t, :], ALPHA, None, ALU.mult).then_inc(s_xs, 1)
            x_rows(0)
            with dve.Fori(0, pairs) as j:
                for u in range(2):
                    dve.wait_ge(s_sg[u], j + 1)
                    v.tensor_tensor(hid[u], ps[:, u, P:2 * P], sg[u], ALU.mult).then_inc(s_h[u], 1)
                dve.wait_ge(s_ht[0], j + 1)
                v.tensor_copy(hT[0], ps[:, 4, 0:P]).then_inc(s_hc[0], 1)
                x_rows(j + 1)
                dve.wait_ge(s_ht[1], j + 1)
                v.tensor_copy(hT[1], ps[:, 4, P:2 * P]).then_inc(s_hc[1], 1)

            dve.wait_ge(s_xs, NT)
            dve.wait_ge(s_ln2, 32)

            def close(t):
                r = rows(t)
                dve.wait_ge(s_nrm2, t + 1)
                v.tensor_tensor(x[0:r, t, :], x[0:r, t, :], lng[0:r, :], ALU.mult).then_inc(s_g2, 1)

            for t in range(NT):
                r = rows(t)
                dve.wait_ge(s_yg[t], 32)
                for k in range(2):
                    link(v.scalar_tensor_tensor(out=x[0:r, t, :], in0=yg[0:r, t, k, :], scalar=wgt[0:r, k, t:t + 1], in1=x[0:r, t, :],
                                                op0=ALU.mult, op1=ALU.add))
                stats(t, s_mv2)
                if t:
                    close(t - 1)
                neg_mean(t, s_rstd2, t + 1)
            close(NT - 1)


_INS = ['x_prompt', 'x_sample', 'cache_k', 'cache_v', 'state_h', 'state_conv', 'page_table',
        'w_in', 'lambda_q1', 'lambda_k1', 'lambda_q2', 'lambda_k2', 'subln_g',
        'conv_w', 'conv_b', 'w_rg_a', 'b_rg_a', 'w_rg_x', 'b_rg_x', 'lru_lambda', 'w_out',
        'ln1_g', 'ln1_b', 'w_group_router', 'b_group_router', 'w_expert_router', 'b_expert_router',
        'w_gate_e', 'w_up_e', 'w_down_e', 'ln2_g', 'ln2_b']
_OUTS = [('y_prompt', (1, SEQ, D)), ('y_sample', (NB, SD, D)),
         ('k_prompt', (1, 1, SEQ, NH, P)), ('v_prompt', (1, 1, SEQ, NH, P)),
         ('h_prompt', (1, 1, W)), ('conv_prompt', (1, 1, 3, W)),
         ('k_sample', (1, NB, SD, NH, P)), ('v_sample', (1, NB, SD, NH, P)),
         ('h_sample', (1, NB, W)), ('conv_sample', (1, NB, 3, W))]


def kernel(**inputs):
    import numpy as _np
    import concourse.bacc as _bacc
    from concourse import mybir as _mybir
    from concourse.bass_utils import run_bass_kernel_spmd as _run

    nc = _bacc.Bacc("TRN2", target_bir_lowering=False, num_devices=1)
    arrays, ins, outs = {}, {}, {}
    for name in _INS:
        a = _np.ascontiguousarray(inputs[name])
        arrays[f"in_{name}_dram"] = a
        ins[name] = nc.dram_tensor(f"in_{name}_dram", a.shape, _mybir.dt.from_np(a.dtype), kind="ExternalInput").ap()
    for name, shape in _OUTS:
        outs[name] = nc.dram_tensor(f"out_{name}_dram", shape, _mybir.dt.float32, kind="ExternalOutput").ap()
    build(nc, ins, outs)
    r = _run(nc, [arrays], core_ids=[0])
    return tuple(r.results[0][f"out_{name}_dram"] for name, _ in _OUTS)
```

```python
from contextlib import ExitStack

import concourse.bass as bass
from concourse import mybir

F32, I32 = mybir.dt.float32, mybir.dt.int32
BF16 = mybir.dt.bfloat16
ALU, ACT, AX = mybir.AluOpType, mybir.ActivationFunctionType, mybir.AxisListType

P = 128
D, SEQ, NB, SD, PAST, PAGE = 1024, 512, 8, 8, 1024, 128
NPG = PAST // PAGE
TS = NB * SD
T = SEQ + TS
NT = (T + P - 1) // P
KD = D // P
NH, W = 4, 512
IN_W = 5 * W
NBLK, BLK = 8, 64
HALF = T // 2
XSEG = SEQ + 3
SSEG = SD + 3
XLW = XSEG + NB * SSEG
NG, EPG, NE, FE = 4, 8, 32, 256
CAP = 64
RING = 3
PAIR0 = NE // 2
PAIRS = PAIR0 + 9
NPAIR = PAIRS + 1
ROUND0, ROUNDS = PAIR0 // RING, PAIRS // RING
TAB0 = 2 * RING * (ROUND0 - 1)
NEXTRA = 2 * PAIRS - NE
I_PAIRS, I_TAB = 0, 1
I_FULL = I_TAB + 2 * PAIRS - TAB0
I_REST, I_PREV = I_FULL + 1, I_FULL + RING
MOREQ = 8
ALPHA, EPS, LRU_C = 2.0 ** 0.25, 1e-5, 8.0
LAM_INIT = 0.8 - 0.6
NEG = -1e30

GUW, DW = 2 * KD * FE, 2 * D
TILEW = GUW + DW
A_XT = 0
A_V = 0
A_XL = 4608
A_LRU = A_XL + 4 * XLW + 4
A_TMP = A_XL
A_KT, A_PE, A_PT, A_V1 = A_XL, A_XL + 4 * 1152, A_XL + 6 * 1152, A_XL + 7 * 1152
A_VN = 18560
A_BD = A_VN + NT * W
A_STG = A_BD + 2 * 4 * P
A_MSK = A_STG + 4 * W
A_WIN = 2 * 2 * TILEW
A_CAT = A_WIN + 2 * KD * W
A_KN = A_CAT + KD * T
A_QD = A_KN + NH * T
A_MOE = RING * 2 * TILEW
A_X1T = A_MOE
A_QZ = A_QD + NB * NH * 32
A_RT = A_X1T + KD * T
A_X = A_QZ + NH * 2 * SEQ
A_MORE = A_X - 4 * D
A_LN = A_X + NT * D
A_SM = A_LN + 2 * D
A_END = 53180
DVE_SUMS = 2


def build(nc, A, O):
    es = ExitStack()
    with es:
        def sem(name):
            return es.enter_context(nc.semaphore(name))

        arena = es.enter_context(nc.sbuf_tensor("arena", [P, A_END], F32))
        ps = es.enter_context(nc.psum_tensor("ps", [P, 8, 512], F32))
        x1_dram = nc.dram_tensor("x1_rows", (T, D), F32, kind="Internal").ap()
        y_slots = nc.dram_tensor("y_slots", (PAIRS * P, D), F32, kind="Internal").ap()

        def area(at, *dims):
            n = 1
            for d in dims:
                n *= d
            v = arena[:, at:at + n]
            if len(dims) == 2:
                v = v.rearrange("p (a b) -> p a b", b=dims[1])
            if len(dims) == 3:
                v = v.rearrange("p (a b c) -> p a b c", b=dims[1], c=dims[2])
            return v

        top = [A_SM]

        def small(*dims):
            n = 1
            for d in dims:
                n *= d
            at = top[0]
            top[0] += n
            assert top[0] <= A_END, top[0]
            return area(at, *dims)

        rtop = [A_RT]

        def rtemp(*dims):
            n = 1
            for d in dims:
                n *= d
            at = rtop[0]
            rtop[0] += n
            assert rtop[0] <= A_X, rtop[0]
            return area(at, *dims)

        xT = area(A_XT, KD, T)
        win = [area(A_WIN + i * KD * W, KD, W) for i in range(2)]
        xl = area(A_XL, 4, XLW)
        xc, rg, ig, th, hh = [area(A_LRU + i * 4 * T, 4, T) for i in range(5)]
        zeros = area(A_LRU + 16 * T, D)
        bd = area(A_BD, 2, 4, P)
        cat = area(A_CAT, KD, T)
        kTn = area(A_KN, NH, T)
        vn = area(A_VN, NT, W)
        qz = area(A_QZ, NH, 2, SEQ)
        qd = area(A_QD, NB, NH, 32)
        x = area(A_X, NT, D)
        lng, lnb = area(A_LN, D), area(A_LN + D, D)
        kstage = area(A_STG, 2, W)
        rows_in = area(A_STG + 2 * W, W)
        ends_out = area(A_STG + 3 * W, W)
        osb = [area(A_STG + 2 * W, NH, P), area(A_STG, NH, P)]
        osq = area(A_STG + 3 * W, NH, P)
        dmask, bigm, sel = area(A_MSK, P), area(A_MSK + P, 184), area(A_MSK + P + 184, 32)
        assert A_MSK + P + 184 + 32 <= A_WIN
        ioti, iotf = area(A_CAT, 184).bitcast(I32), area(A_CAT + 184, 184)
        sel01 = [area(A_CAT + 368 + i * 32, 32) for i in range(2)]
        lamv = area(A_CAT + 432, 4, BLK)
        pexp = [area(A_TMP + i * 2 * SEQ, 2, SEQ) for i in range(2)]
        wdiff = [area(A_TMP + 4 * SEQ + i * SEQ, SEQ) for i in range(2)]
        wT = [area(A_TMP + 6 * SEQ + i * SEQ, SEQ) for i in range(2)]
        assert A_TMP + 8 * SEQ <= A_V1 and A_V1 + NPG * W <= A_VN and A_LRU + 20 * T <= A_VN
        kpages = [area(A_WIN + i * NPG * W, NPG, W) for i in range(2)]
        vpages = [area(A_V, NPG, W), area(A_V1, NPG, W)]
        kT = area(A_KT, NH, 1152)
        pes = [area(A_PE + i * 1152, 9, P) for i in range(2)]
        pT = area(A_PT, 9, P)
        osm = [area(A_STG + i * P, P) for i in range(2)]
        oTs = area(A_STG + W, NB, 32)
        oTq = area(A_STG + 2 * W, NB, 32)
        oTr = area(A_STG + 3 * W, NB, 32)
        wout = area(A_WIN, KD, D)
        x1T = area(A_X1T, KD, T)
        xg = [area(A_MOE, D), area(A_MORE, D), area(A_MORE + D, D)]
        xTm = area(A_MOE + D, KD, P)
        sg = [area(A_MOE + 2 * D + i * P, P) for i in range(2)]
        hid = [area(A_MOE + 2 * D + (2 + i) * P, P) for i in range(2)]
        hT = [area(A_MOE + 2 * D + (4 + i) * P, P) for i in range(2)]
        ysb = [[area(at + i * W, W) for i in range(2)] for at in (A_MOE + 2 * D + 6 * P, A_MORE + 2 * D, A_MORE + 3 * D)]
        assert A_MOE + 2 * D + 6 * P + 2 * W <= A_MORE
        yg = area(0, NT, 2, D)
        diag = area(A_MOE, 2 * NT, P)
        ident = small(P)
        qcur = small(NH, 32)
        prm = small(4, 40)
        ends = small(4, 36)
        cl = small(4, 4)
        g08 = small(1)
        lex = small(4, 1)
        parti, partf = small(1).bitcast(I32), small(1)
        sc = small(32)
        mx, sm, rc = small(2, 2, NH), small(2, 2, NH), small(2, 2, NH)
        st = small(12)
        mv = small(NT, 2)
        ss = small(NH)
        coef = small(4)
        ptab = small(64).bitcast(I32)
        info = small(48).bitcast(I32)
        idx = small(NPAIR).bitcast(I32)
        icur = small(RING).bitcast(I32)
        yidx = small(2, NT).bitcast(I32)
        wgt = small(2, NT)
        nhalf = small(NT)
        pw = small(NT)

        wr, rbias = rtemp(KD, NG + NE), rtemp(NG + NE)
        ones, tri = rtemp(P), rtemp(P)
        ones16, tri16 = rtemp(P // 2).bitcast(BF16), rtemp(P // 2).bitcast(BF16)
        toklo, tokhi = rtemp(NT), rtemp(NT)
        counts = rtemp(NT * NE // 2).bitcast(BF16)
        io128i, io128f = rtemp(P).bitcast(I32), rtemp(P)
        toki, tokf, valid = rtemp(NT).bitcast(I32), rtemp(NT), rtemp(NT)
        L = rtemp(NT, NG + NE)
        rexp = rtemp(NT, NG + 1)
        gmax, m1, m2 = rtemp(NT), rtemp(NT), rtemp(NT)
        gfirst, efirst = rtemp(NT), rtemp(2, NT)
        goh, oh1, oh2, t8, wi = rtemp(NT, NG), rtemp(NT, EPG), rtemp(NT, EPG), rtemp(NT, EPG), rtemp(NT, EPG)
        ek = rtemp(2 * NT, NE)
        ekx = rtemp(2 * NT, NE)
        ohs, rank = rtemp(NT, NE), rtemp(NT, NE)
        run, more, before, upto = rtemp(NE), rtemp(NE), rtemp(NE), rtemp(NE)
        capt, pairt = rtemp(MOREQ), rtemp(NPAIR - 1)
        rk, rb, re_, rf, rs = [rtemp(2 * NT) for _ in range(5)]
        one = rtemp(4)
        posoh = area(A_X1T, NT * P).bitcast(BF16).rearrange("p (n c) -> p n c", c=P)
        at = A_X1T + 2 * NT * P
        assert A_MOE + D <= at
        pairoh = area(at, 2 * NT, NPAIR)
        cmp8 = area(at + 2 * NT * NPAIR, 2 * NT, NPAIR)
        at += 4 * NT * NPAIR
        pairlo, pairhi = [area(at + i * NT * NPAIR, NT * NPAIR).bitcast(BF16).rearrange("p (n c) -> p n c", c=NPAIR) for i in range(2)]
        at = A_RT - NEXTRA * (NE + 1)
        assert at >= A_MOE + 2 * D + 6 * P + 2 * W
        xsel, xexp = area(at, NEXTRA, NE), area(at + NEXTRA * NE, NEXTRA)
        assert RING == 3 and I_PREV < 48 and 2 * T // (CAP + 1) <= NEXTRA

        s_x = [sem(f"x_in{t}") for t in range(NT)]; s_win0 = sem("w_in_first_half"); s_win = [sem(f"w_in{i}") for i in range(2)]
        s_par = sem("params_in"); s_bdin = sem("gate_blocks_in"); s_pt = sem("page_table_in")
        s_cst = sem("constants"); s_ln1 = sem("ln1_and_lambdas_in"); s_rt = sem("router_in"); s_lc = sem("late_constants")
        s_le = sem("lru_exp_in"); s_lex = sem("lru_exp"); s_lexp = sem("lambda_exp"); s_mvn = sem("ln_bias"); s_sch = sem("sample_chain"); s_msk = sem("sample_mask"); s_dc = sem("dve_constants")
        s_xtp = sem("x_transposed"); s_xe = [sem(f"xT_half{i}") for i in range(2)]
        s_pj = sem("projected"); s_pev = [sem(f"proj_bank{i}_read") for i in range(2)]
        s_rows = sem("param_rows_transposed"); s_prm = sem("params_ready")
        s_xc = sem("conv_done"); s_lam = sem("lru_rate")
        s_th = sem("tanh_done"); s_m2 = sem("mult2_done"); s_mult = sem("mult_done")
        s_ends = sem("ends_ready"); s_endp = sem("ends_transposed"); s_endc = sem("ends_rows")
        s_kt = sem("k_rows_psum"); s_kc = sem("k_rows_sbuf")
        s_kout = [sem(f"k_out{i}") for i in range(2)]
        s_out = sem("small_outputs"); s_ch = sem("dve_chain"); s_pch = sem("pool_chain")
        s_sp = sem("prompt_scores"); s_mxp = sem("prompt_max"); s_exp = sem("prompt_exp")
        s_w = sem("prompt_weights"); s_wt = sem("weights_transposed"); s_wc = sem("wT_ready")
        s_pvp = sem("prompt_values"); s_oc = sem("o_copied"); s_var = sem("rms_in")
        s_rs = sem("rms_out"); s_on = sem("o_normed"); s_ot = sem("o_transposed"); s_oe = sem("o_in_cat")
        s_kin = [sem(f"keys_in{i}") for i in range(2)]; s_vin = [sem(f"values_in{i}") for i in range(2)]
        s_ktp = [sem(f"keys_transposed{i}") for i in range(2)]
        s_ktc = [sem(f"kT_bank{i}_read") for i in range(2)]
        s_qc = sem("query_block"); s_sc = sem("sample_scores"); s_mxs = sem("sample_max")
        s_exs = sem("sample_exp"); s_ptp = sem("probs_transposed"); s_pta = sem("pT_by_act"); s_ptd = sem("pT_by_dve")
        s_pvs = sem("sample_values"); s_os = sem("o_scaled"); s_cmb = sem("maps_combined"); s_oct = sem("combined_read")
        s_sq = sem("o_squared"); s_sqm = sem("square_sums"); s_srs = sem("sample_rms"); s_cat = sem("cat_done")
        s_wo = sem("w_out_in"); s_op = sem("merged"); s_opr = sem("merge_bank_read")
        s_mv = sem("ln_stats"); s_rstd = sem("ln_rstd"); s_x1 = sem("x1_ready")
        s_x1d = sem("x1_stored"); s_x1t = sem("x1_transposed"); s_x1e = [sem(f"x1T_half{i}") for i in range(2)]
        s_lgt = sem("logits_psum")
        s_ln2 = sem("ln2_params_in")
        s_re = sem("route_exp_in"); s_rx = sem("route_exp"); s_oh = sem("choice_onehots"); s_rk = sem("ranks_psum")
        s_ab = sem("slot_onehots"); s_tab = sem("slot_table_psum"); s_idx = sem("slot_table_ready"); s_xinfo = sem("further_experts"); s_info = sem("routing_done")
        s_wgu = [[sem(f"w_gate_up{i}_{u}") for u in range(2)] for i in range(RING)]
        s_wd = [[sem(f"w_down{i}_{u}") for u in range(2)] for i in range(RING)]
        s_gi = sem("gather_index"); s_gx = [sem(f"rows_gathered{i}") for i in range(RING)]; s_xt = sem("rows_transposed")
        s_xa = sem("xTm_half0"); s_xd = sem("xTm_half1")
        s_gu = [sem(f"gate_up{i}") for i in range(2)]; s_sg = [sem(f"silu{i}") for i in range(2)]
        s_h = [sem(f"hidden{i}") for i in range(2)]; s_ht = [sem(f"hidden_T{i}") for i in range(2)]
        s_hc = [sem(f"hT_ready{i}") for i in range(2)]; s_y = [sem(f"down{i}") for i in range(2)]
        s_yc = [sem(f"y_copied{i}") for i in range(2)]; s_yd = [sem(f"y_stored{i}") for i in range(RING)]
        s_diag = sem("weights_on_diagonals"); s_yw = sem("rows_weighed")
        s_yg = [sem(f"y_gathered{i}") for i in range(NT)]
        s_mv2 = sem("ln2_stats"); s_rstd2 = sem("ln2_rstd"); s_nrm2 = sem("ln2_scaled"); s_g2 = sem("ln2_gained")
        s_turn = sem("pool_turns"); s_sturn = sem("sync_turns"); s_zero = sem("zeros"); s_fill = sem("spare_slots_filled")
        s_fin = sem("result_ready"); s_last = sem("last_tile_ready"); s_res = sem("result_stored")

        def rows(t):
            return P if t < NT - 1 else TS

        XL, GL, Q, K_, V_ = 3, 4, 0, 1, 2
        ORDER = [XL, GL, Q, K_, V_]
        w_in = A["w_in"][0]

        STEPS = []
        for i in range(NT - 1):
            n = min(NH, W // ((i + 1) * P))
            STEPS += [(i, range(h, h + n)) for h in range(0, NH, n)]
        ends_tile = [max(n for n, (j, _) in enumerate(STEPS) if j == i) for i in range(NT - 1)]

        def tile_ended(n, after):
            return ends_tile.index(n - after) if n - after in ends_tile else None

        def moe_pairs(engine):
            return engine.value_load(info[0:1, I_PAIRS:I_PAIRS + 1], min_val=PAIR0, max_val=PAIRS)

        def full_rounds(engine, further=0):
            return engine.value_load(info[0:1, I_FULL:I_FULL + 1], min_val=ROUND0, max_val=(PAIRS - further) // RING)

        def moe_size(engine):
            return full_rounds(engine), [engine.value_load(info[0:1, I_REST + n:I_REST + n + 1], min_val=0, max_val=1) for n in range(RING - 1)]

        block = es.enter_context(nc.Block())

        @block.sync
        def _(sp):
            for t in range(NT - 1):
                sp.dma_start(x[:, t, :], A["x_prompt"][0, t * P:(t + 1) * P, :]).then_inc(s_x[t], 16)
            sp.dma_start(x[0:TS, NT - 1, :], A["x_sample"].rearrange("b s d -> (b s) d")).then_inc(s_x[NT - 1], 16)
            for n, c in enumerate(ORDER):
                if n >= 2:
                    sp.wait_ge(s_pj, [4, 8, 20][n - 2])
                src = w_in[:, c * W:(c + 1) * W].rearrange("(k p) n -> p k n", p=P)
                if n == 0:
                    sp.dma_start(win[0][:, 0:KD // 2, :], src[:, 0:KD // 2, :]).then_inc(s_win0, 16)
                    src, at = src[:, KD // 2:, :], KD // 2
                else:
                    at = 0
                sp.dma_start(win[n % 2][:, at:, :], src).then_inc(s_win[n % 2], 16)

            ck = A["cache_k"][0].rearrange("n s h d -> (n s) (h d)")
            n_phys = A["cache_k"].shape[1]
            sp.wait_ge(s_pt, 16)

            def keys(b, u, ready):
                at = [sp.value_load(ptab[0:1, bass.ds(b * NPG + g, 1)], min_val=0, max_val=n_phys - 1) for g in range(NPG)]
                ready()
                for g in range(NPG):
                    sp.dma_start(kpages[u][:, g, :], ck[bass.ds(at[g] * PAGE, PAGE), :]).then_inc(s_kin[u], 16)

            keys(0, 0, lambda: sp.wait_ge(s_pj, 29))
            keys(1, 1, lambda: None)
            with sp.Fori(1, NB // 2) as jb:
                for u in range(2):
                    b = 2 * jb + u

                    def keys_free():
                        sp.wait_ge(s_ktp[1], 4 * b - 4)
                        sp.sem_inc(s_sturn, 1)

                    keys(b, u, keys_free)

            sp.wait_ge(s_ktp[1], 4 * NB)
            sp.dma_start(wout[:, :, :], A["w_out"][0].rearrange("(k p) n -> p k n", p=P)).then_inc(s_wo, 16)

            wg = A["w_gate_e"][0].rearrange("e d f -> (e d) f")
            wu = A["w_up_e"][0].rearrange("e d f -> (e d) f")
            wd = A["w_down_e"][0].rearrange("e f d -> (e f) d")

            def load_gate_up(e, at, done):
                sp.dma_start(arena[:, at:at + GUW // 2], wg[bass.ds(e * D, D), :].rearrange("(p k) f -> p (k f)", p=P)).then_inc(done, 16)
                sp.dma_start(arena[:, at + GUW // 2:at + GUW], wu[bass.ds(e * D, D), :].rearrange("(p k) f -> p (k f)", p=P)).then_inc(done, 16)

            def load_down(e, at, done):
                sp.dma_start(area(at, 2, D), wd[bass.ds(e * FE, FE), :].rearrange("(a p) d -> p a d", p=P)).then_inc(done, 16)

            sp.wait_ge(s_cat, 1)
            sp.wait_ge(s_out, 16 * 6)
            sp.wait_ge(s_kout[0], 16 * 3)
            sp.wait_ge(s_kout[1], 16 * 2)
            for slot in range(RING):
                if slot == RING - 1:
                    sp.wait_ge(s_op, NT)
                for u in range(2):
                    at = (2 * slot + u) * TILEW
                    load_gate_up(2 * slot + u, at, s_wgu[slot][u])
                    load_down(2 * slot + u, at + GUW, s_wd[slot][u])

            def next_pair(prev, slot, expert):
                experts = [expert(u) for u in range(2)]
                for u in range(2):
                    sp.wait_ge(s_gu[u], RING * prev + slot + 1)
                    sp.sem_inc(s_sturn, 1)
                    load_gate_up(experts[u], (2 * slot + u) * TILEW, s_wgu[slot][u])
                for u in range(2):
                    sp.wait_ge(s_y[u], RING * prev + slot + 1)
                    sp.sem_inc(s_sturn, 1)
                    load_down(experts[u], (2 * slot + u) * TILEW + GUW, s_wd[slot][u])

            with sp.Fori(0, ROUND0 - 2) as prev:
                for slot in range(RING):
                    next_pair(prev, slot, lambda u: 2 * RING * (prev + 1) + 2 * slot + u)

            def from_table(prev, slot):
                next_pair(prev, slot, lambda u: sp.value_load(
                    info[0:1, bass.ds(2 * RING * (prev - (ROUND0 - 2)) + 2 * slot + u + I_TAB, 1)], min_val=0, max_val=NE - 1))

            sp.wait_ge(s_info, 1)
            sp.wait_ge(s_xinfo, 1)
            _, rest = moe_size(sp)
            with sp.Fori(ROUND0 - 2, sp.value_load(info[0:1, I_PREV:I_PREV + 1], min_val=ROUND0 - 1, max_val=ROUNDS - 1)) as prev:
                for slot in range(RING):
                    from_table(prev, slot)
            for slot in range(RING - 1):
                with sp.If(rest[slot] > 0):
                    from_table(sp.value_load(info[0:1, I_PREV:I_PREV + 1], min_val=ROUND0 - 1, max_val=(PAIRS - slot - 1) // RING - 1), slot)

            for t in range(NT):
                if t < NT - 1:
                    sp.wait_ge(s_fin, t + 1)
                    sp.dma_start(O["y_prompt"][0, t * P:(t + 1) * P, :], x[:, t, :]).then_inc(s_res, 16)
                else:
                    sp.wait_ge(s_last, 1)
                    sp.dma_start(O["y_sample"].rearrange("b s d -> (b s) d"), x[0:TS, t, :]).then_inc(s_res, 16)
            sp.wait_ge(s_res, 16 * NT)

        @block.gpsimd
        def _(q):
            def pool_link(ins, state=[0]):
                state[0] += 1
                ins.then_inc(s_pch, 1)
                q.wait_ge(s_pch, state[0])

            g = nc.gpsimd
            pool_link(g.memset(ident, 0.0))
            g.affine_select(out=ident, in_=ident, compare_op=ALU.not_equal, fill=1.0, base=0,
                            pattern=[[-1, P]], channel_multiplier=1).then_inc(s_cst, 1)
            g.memset(rows_in, 0.0).then_inc(s_cst, 1)
            q.wait_ge(s_cst, 2)
            q.dma_start(rows_in[0:4, :], A["conv_w"][0]).then_inc(s_par, 16)
            for at, name in ((4, "conv_b"), (7, "lru_lambda")):
                q.dma_start(rows_in[at:at + 1, :], A[name][0:1, :]).then_inc(s_par, 16)
            for at, name in ((5, "b_rg_a"), (6, "b_rg_x")):
                q.dma_start(rows_in[at:at + 1, :], A[name].rearrange("o n b -> o (n b)")).then_inc(s_par, 16)
            q.dma_start(rows_in[8:16, :], A["state_h"][0]).then_inc(s_par, 16)
            q.dma_start(rows_in[16:40, :], A["state_conv"][0].rearrange("b j c -> (b j) c")).then_inc(s_par, 16)
            pool_link(g.memset(bd, 0.0))
            g.memset(zeros, 0.0).then_inc(s_zero, 1)
            for n, name in enumerate(("w_rg_a", "w_rg_x")):
                src = A[name][0].rearrange("(t u) i j -> u i t j", u=2)
                for u in range(2):
                    q.dma_start(bd[u * BLK:(u + 1) * BLK, n, :, u * BLK:(u + 1) * BLK], src[u]).then_inc(s_bdin, 16)
            pool_link(g.memset(qd, 0.0))
            pool_link(g.memset(qz, 0.0))
            pool_link(g.memset(xl[:, :, 0:3], 0.0))
            pool_link(g.memset(vn[:, NT - 1, :], 0.0))
            pool_link(g.memset(dmask, 0.0))
            pool_link(g.affine_select(out=dmask, in_=dmask, compare_op=ALU.is_ge, fill=NEG, base=0,
                                      pattern=[[-1, P]], channel_multiplier=1))
            for m, s in enumerate(sel01):
                pool_link(g.memset(s, 0.0))
                v = s.rearrange("p (h q) -> p h q", q=SD)
                pool_link(g.affine_select(out=v, in_=v, compare_op=ALU.not_equal, fill=1.0, base=-SD * m,
                                          pattern=[[-32, NH], [-1, SD]], channel_multiplier=1))
            pool_link(g.iota(ioti, pattern=[[1, 184]], base=-56, channel_multiplier=0))
            pool_link(g.iota(parti, pattern=[[0, 1]], base=0, channel_multiplier=1))
            g.memset(nhalf, -0.5).then_inc(s_cst, 1)

            cv = A["cache_v"][0].rearrange("n s h d -> (n s) (h d)")
            n_phys = A["cache_v"].shape[1]

            def values(b, u, ready):
                at = [q.value_load(ptab[0:1, bass.ds(b * NPG + g, 1)], min_val=0, max_val=n_phys - 1) for g in range(NPG)]
                ready()
                for g_ in range(NPG):
                    q.dma_start(vpages[u][:, g_, :], cv[bass.ds(at[g_] * PAGE, PAGE), :]).then_inc(s_vin[u], 16)

            for t in range(NT):
                q.wait_ge(s_kc, t + 1)
                if t < NT - 1:
                    dst = O["k_prompt"][0, 0, t * P:(t + 1) * P].rearrange("s h d -> s (h d)")
                else:
                    dst = O["k_sample"][0].rearrange("b s h d -> (b s) (h d)")
                q.dma_start(dst, kstage[0:rows(t), t % 2, :]).then_inc(s_kout[t % 2], 16)
            q.wait_ge(s_pev[0], 30)
            q.wait_ge(s_pev[1], 28)
            q.dma_start(O["v_prompt"][0, 0].rearrange("(t p) h d -> p t (h d)", p=P), vn[:, 0:NT - 1, :]).then_inc(s_out, 16)
            q.dma_start(O["v_sample"][0].rearrange("b s h d -> (b s) (h d)"), vn[0:TS, NT - 1, :]).then_inc(s_out, 16)
            q.wait_ge(s_pt, 16)
            values(0, 0, lambda: q.wait_ge(s_pj, 29))
            q.wait_ge(s_endc, 1)
            q.dma_start(O["h_prompt"][0], ends_out[0:1, :]).then_inc(s_out, 16)
            q.dma_start(O["h_sample"][0], ends_out[1:9, :]).then_inc(s_out, 16)
            q.dma_start(O["conv_prompt"][0, 0], ends_out[9:12, :]).then_inc(s_out, 16)
            q.dma_start(O["conv_sample"][0].rearrange("b j c -> (b j) c"), ends_out[12:36, :]).then_inc(s_out, 16)

            values(1, 1, lambda: q.wait_ge(s_ends, 1))

            for i in range(NT - 1):
                q.wait_ge(s_var, i + 1)
                g.tensor_tensor(ss, ss, nhalf[:, 0:NH], ALU.pow).then_inc(s_rs, 1)

            def query(b):
                q.wait_ge(s_sc, b)
                q.wait_ge(s_cst, 3)
                g.tensor_copy(qcur, qd[:, b, :, :] if isinstance(b, int) else
                              arena[:, bass.ds(A_QD + b * (NH * 32), NH * 32)].rearrange("p (h c) -> p h c", h=NH)).then_inc(s_qc, 1)

            q.wait_ge(s_sp, len(STEPS))
            g.memset(ones, 1.0).then_inc(s_lc, 1)
            g.memset(tri, 1.0).then_inc(s_lc, 1)
            q.wait_ge(s_lc, 2)
            g.affine_select(out=tri, in_=tri, compare_op=ALU.is_gt, fill=0.0, base=0, pattern=[[1, P]], channel_multiplier=-1).then_inc(s_lc, 1)
            g.iota(io128i, pattern=[[1, P]], base=0, channel_multiplier=0).then_inc(s_lc, 1)
            g.iota(toki, pattern=[[P, NT]], base=0, channel_multiplier=1).then_inc(s_lc, 1)
            g.tensor_copy(qcur, qd[:, 0, :, :]).then_inc(s_qc, 1)
            query(1)
            with q.Fori(1, NB // 2) as jb:
                for u in range(2):
                    b = 2 * jb + u

                    def values_free():
                        q.wait_ge(s_pvs, b - 1)
                        q.sem_inc(s_turn, 1)

                    values(b, u, values_free)
                    query(b)

            for t in range(NT):
                q.wait_ge(s_mv, t + 1)
                g.tensor_tensor(pw[:, t:t + 1], pw[:, t:t + 1], nhalf[:, 0:1], ALU.pow).then_inc(s_rstd, 1)

            q.wait_ge(s_idx, 1)
            q.wait_ge(s_x1d, 16 * NT)

            def gather(slot, j):
                g.tensor_copy(icur[:, slot:slot + 1], idx[:, bass.ds(j, 1)]).then_inc(s_gi, 1)
                q.wait_ge(s_gi, j + 1)
                q.sem_inc(s_turn, 1)
                q.indirect_dma_start(out=xg[slot], out_offset=None, in_=x1_dram,
                                     in_offset=bass.IndirectOffsetOnAxis(ap=icur[:, slot:slot + 1], axis=0)).then_inc(s_gx[slot], 16)

            def next_gather(prev, slot):
                q.wait_ge(s_xt, 2 * (RING * prev + slot) + 2)
                q.wait_ge(s_gx[slot], 16 * prev + 16)
                q.wait_ge(s_info, 1)
                gather(slot, RING * prev + RING + slot)

            gather(0, 0)
            q.wait_ge(s_info, 1)
            q.wait_ge(s_xinfo, 1)
            for slot in range(1, RING):
                gather(slot, slot)
            full, rest = moe_size(q)

            def last_full(further):
                return q.value_load(info[0:1, I_PREV:I_PREV + 1], min_val=ROUND0 - 1, max_val=(PAIRS - further) // RING - 1)

            with q.Fori(0, last_full(0)) as prev:
                for slot in range(RING):
                    next_gather(prev, slot)
            next_gather(last_full(0), 0)
            for slot in range(1, RING):
                with q.If(rest[slot - 1] > 0):
                    next_gather(last_full(slot), slot)

            q.wait_ge(s_fill, 16 * (PAIRS - PAIR0))
            for slot in range(RING):
                q.wait_ge(s_yd[slot], 64 * full + 64 * rest[slot] if slot < RING - 1 else 64 * full)
            q.sem_inc(s_turn, 1)
            for t in range(NT):
                r = rows(t)
                for k in range(2):
                    q.indirect_dma_start(out=yg[0:r, t, k, :], out_offset=None, in_=y_slots,
                                         in_offset=bass.IndirectOffsetOnAxis(ap=yidx[0:r, k, t:t + 1], axis=0)).then_inc(s_yg[t], 16)
            for t in range(NT):
                r = rows(t)
                q.wait_ge(s_mv2, t + 1)
                g.tensor_tensor(pw[:, t:t + 1], pw[:, t:t + 1], nhalf[:, 0:1], ALU.pow).then_inc(s_rstd2, 1)
                if t:
                    q.wait_ge(s_g2, t)
                    g.tensor_tensor(x[:, t - 1, :], x[:, t - 1, :], lnb, ALU.add).then_inc(s_fin, 1)

        def o_transpose(pe, i):
            pe.wait_ge(s_on, i + 1)
            if i:
                pe.wait_ge(s_oe, i)
            for h in range(NH):
                last = nc.tensor.transpose(ps[:, 7, h * P:(h + 1) * P], osb[i % 2][:, h, :], ident)
            last.then_inc(s_ot, 1)

        @block.tensor
        def _(pe):
            mm, tr = nc.tensor.matmul, nc.tensor.transpose
            pe.wait_ge(s_cst, 1)
            for t in range(NT):
                pe.wait_ge(s_x[t], 16)
                for half in range(2):
                    n = 2 * t + half
                    if n >= 2:
                        pe.wait_ge(s_xe[half], t)
                    for kk in range(4):
                        k = 4 * half + kk
                        last = tr(ps[:, 4 + half, kk * P:kk * P + rows(t)], x[0:rows(t), t, k * P:(k + 1) * P], ident[0:rows(t), 0:rows(t)])
                    last.then_inc(s_xtp, 1)
            for h in range(2):
                pe.wait_ge(s_xe[h], NT)

            unit = [0]

            def bank_free():
                n = unit[0]
                unit[0] += 1
                if n >= 2:
                    pe.wait_ge(s_pev[n % 2], 2 * (n // 2))
                return 2 * (n % 2)

            def k_rows(t):
                if t >= 2:
                    pe.wait_ge(s_kc, t - 1)
                for h in range(NH):
                    last = tr(ps[0:rows(t), 4 + t % 2, h * P:(h + 1) * P], kTn[:, h, t * P:t * P + rows(t)], ident)
                last.then_inc(s_kt, 1)

            for n, c in enumerate(ORDER):
                if n:
                    pe.wait_ge(s_win[n % 2], 16 * (n // 2 + 1))
                if c != V_:
                    for m in range(4):
                        b = bank_free()
                        for k in range(KD):
                            if n == 0 and m == 0 and k % (KD // 2) == 0:
                                pe.wait_ge((s_win0, s_win[0])[k // (KD // 2)], 16)
                            for h in range(2):
                                last = mm(ps[:, b + h, 0:HALF], win[n % 2][:, k, m * P:(m + 1) * P], xT[:, k, h * HALF:(h + 1) * HALF],
                                          start=k == 0, stop=k == KD - 1)
                        last.then_inc(s_pj, 1)
                        if n == 0 and m == 0:
                            pe.wait_ge(s_par, 16 * 7)
                            for t in range(4):
                                last = tr(ps[:, 6, t * 40:(t + 1) * 40], rows_in[0:40, t * P:(t + 1) * P], ident[0:40, 0:40])
                            last.then_inc(s_rows, 1)
                else:
                    for t in range(NT):
                        b = bank_free()
                        for k in range(KD):
                            if t < NT - 1:
                                last = mm(ps[:, b, :], xT[:, k, t * P:(t + 1) * P], win[n % 2][:, k, :], start=k == 0, stop=k == KD - 1)
                            else:
                                for h in range(2):
                                    last = mm(ps[h * TS:(h + 1) * TS, b + h, 0:W // 2], xT[:, k, t * P:T], win[n % 2][:, k, h * W // 2:(h + 1) * W // 2],
                                              start=k == 0, stop=k == KD - 1)
                        last.then_inc(s_pj, 1)
                        if t == 0:
                            for h in range(2):
                                pe.wait_ge(s_pev[h], 24)
                        k_rows(t)
                if c == GL:
                    pe.wait_ge(s_bdin, 64)
                    for t in range(4):
                        pe.wait_ge(s_xc, t + 1)
                        for a in range(2):
                            b = bank_free()
                            for h in range(2):
                                last = mm(ps[:, b + h, 0:HALF], bd[:, a, t, :], xc[:, t, h * HALF:(h + 1) * HALF], start=True, stop=True)
                            last.then_inc(s_pj, 1)
            for h in range(2):
                pe.wait_ge(s_pev[h], 30 - 2 * h)
            pe.wait_ge(s_ends, 1)
            for t in range(4):
                last = tr(ps[0:36, 6, t * P:(t + 1) * P], ends[:, t, :], ident)
            last.then_inc(s_endp, 1)

            pe.wait_ge(s_kc, NT)
            pe.wait_ge(s_endc, 1)
            def scores(n):
                i, heads = STEPS[n]
                w = (i + 1) * P
                if n >= 2:
                    pe.wait_ge(s_exp, n - 1)
                for m in range(2):
                    for j, h in enumerate(heads):
                        last = mm(ps[:, 2 * (n % 2) + m, j * w:(j + 1) * w], qz[:, h, m, i * P:(i + 1) * P], kTn[:, h, 0:w], start=True, stop=True)
                last.then_inc(s_sp, 1)

            def transposes(n):
                i, heads = STEPS[n]
                pe.wait_ge(s_w, n + 1)
                if n >= 2:
                    pe.wait_ge(s_wc, n - 1)
                for kt in range(len(heads) * (i + 1)):
                    last = tr(ps[:, 4 + n % 2, kt * P:(kt + 1) * P], wdiff[n % 2][:, kt * P:(kt + 1) * P], ident)
                last.then_inc(s_wt, 1)

            def values(n):
                i, heads = STEPS[n]
                pe.wait_ge(s_wc, n + 1)
                if heads[0] == 0 and i:
                    pe.wait_ge(s_oc, i)
                for j, h in enumerate(heads):
                    for kt in range(i + 1):
                        at = j * (i + 1) + kt
                        last = mm(ps[:, 6, h * P:(h + 1) * P], wT[n % 2][:, at * P:(at + 1) * P], vn[:, kt, h * P:(h + 1) * P],
                                  start=kt == 0, stop=kt == i)
                last.then_inc(s_pvp, 1)

            scores(0)
            scores(1)
            scores(2)
            transposes(0)
            for n in range(len(STEPS)):
                if n + 3 < len(STEPS):
                    scores(n + 3)
                if n + 1 < len(STEPS):
                    transposes(n + 1)
                values(n)
                if tile_ended(n, 3) is not None:
                    o_transpose(pe, tile_ended(n, 3))

            pe.wait_ge(s_exp, len(STEPS))
            pe.wait_ge(s_wc, len(STEPS))

            def keys_transpose(b, u, g, first=False):
                if g == 0:
                    pe.wait_ge(s_kin[u], (b - u) * (P // 2) + P)
                if not (first and g < 2):
                    pe.wait_ge(s_ktc[g % 2], 4 * b + g // 2)
                for h in range(NH):
                    last = tr(ps[:, 3 + g % 2, h * P:(h + 1) * P], kpages[u][:, g, h * P:(h + 1) * P], ident)
                last.then_inc(s_ktp[g % 2], 1)

            def sample_scores(b):
                pe.wait_ge(s_qc, b + 1)
                pe.wait_ge(s_ktc[0], 4 * b + 4)
                pe.wait_ge(s_ktc[1], 4 * b + 4)
                pe.wait_ge(s_exs, b)
                pe.wait_ge(s_cst, 3)
                for c in range(3):
                    for h in range(NH):
                        last = mm(ps[32 * h:32 * h + 32, c, 0:384], qcur[:, h, :], kT[:, h, c * 384:(c + 1) * 384], start=True, stop=True)
                last.then_inc(s_sc, 1)

            def probs_transpose(b, u, grp):
                k0, k1 = ((0, 4), (4, 8), (8, 9))[grp]
                if grp == 0:
                    pe.wait_ge(s_exs, b + 1)
                if grp == 2:
                    pe.wait_ge(s_pta, 2 * b + 1)
                for kt in range(k0, k1):
                    last = tr(ps[:, 5 + grp % 2, (kt - k0) * P:(kt - k0 + 1) * P], pes[u][:, kt, :], ident)
                last.then_inc(s_ptp, 1)

            def sample_values(b, u, k0, k1):
                if k0 == 0:
                    pe.wait_ge(s_vin[u], (b - u) * (P // 2) + P)
                    pe.wait_ge(s_pta, 2 * b + 2)
                    pe.wait_ge(s_ptd, b + 1)
                for kt in range(k0, k1):
                    for h in range(NH):
                        v = vpages[u][:, kt, h * P:(h + 1) * P] if kt < 8 else vn[:, NT - 1, h * P:(h + 1) * P]
                        last = mm(ps[32 * h:32 * h + 32, 7, 0:P], pT[:, kt, 32 * h:32 * h + 32], v, start=kt == 0, stop=kt == 8)
                if k1 == 9:
                    last.then_inc(s_pvs, 1)

            def combine(b, u):
                pe.wait_ge(s_os, b + 1)
                if not (isinstance(b, int) and b == 0):
                    pe.wait_ge(s_oct, b)
                mm(ps[:, 7, 256:288], osm[u], sel, start=True, stop=True).then_inc(s_cmb, 1)

            def sample(b, u, first=False, last=False):
                if not first:
                    combine(b - 1, 1 - u)
                if not last:
                    for g in range(4):
                        keys_transpose(b + 1, 1 - u, g)
                probs_transpose(b, u, 0)
                probs_transpose(b, u, 1)
                if not last:
                    keys_transpose(b + 1, 1 - u, 4)
                    keys_transpose(b + 1, 1 - u, 5)
                probs_transpose(b, u, 2)
                if not last:
                    keys_transpose(b + 1, 1 - u, 6)
                sample_values(b, u, 0, 5)
                if not last:
                    keys_transpose(b + 1, 1 - u, 7)
                sample_values(b, u, 5, 9)
                if not last:
                    sample_scores(b + 1)

            for g in range(NPG):
                keys_transpose(0, 0, g, True)
            o_transpose(pe, NT - 2)
            pe.wait_ge(s_dc, 2)
            sample_scores(0)
            pe.wait_ge(s_oe, NT - 1)
            sample(0, 0, first=True)
            with pe.Fori(0, NB // 2 - 1) as jb:
                sample(2 * jb + 1, 1)
                sample(2 * jb + 2, 0)
            sample(NB - 1, 1, last=True)
            combine(NB - 1, 1)
            def squares():
                pe.wait_ge(s_lc, 5)
                pe.wait_ge(s_sq, 1)
                mm(ps[:, 6, 0:NB * 32], ones, oTq.rearrange("p b c -> p (b c)"), start=True, stop=True).then_inc(s_sqm, 1)

            pe.wait_ge(s_wo, 16)

            def x1_transpose(t):
                pe.wait_ge(s_x1, t + 1)
                for half in range(2):
                    if t:
                        pe.wait_ge(s_x1e[half], t)
                    for kk in range(4):
                        k = 4 * half + kk
                        last = tr(ps[:, 4 + half, kk * P:kk * P + rows(t)], x[0:rows(t), t, k * P:(k + 1) * P], ident[0:rows(t), 0:rows(t)])
                    last.then_inc(s_x1t, 1)

            def logits(t):
                if t == 0:
                    pe.wait_ge(s_rt, 64)
                for h in range(2):
                    pe.wait_ge(s_x1e[h], t + 1)
                for k in range(KD):
                    last = mm(ps[0:rows(t), 6, t * 36:t * 36 + 36], x1T[:, k, t * P:t * P + rows(t)], wr[:, k, :], start=k == 0, stop=k == KD - 1)
                last.then_inc(s_lgt, 1)

            for t in range(NT):
                if t >= 2:
                    pe.wait_ge(s_opr, t - 1)
                if t < NT - 1:
                    for h in range(2):
                        for k in range(KD):
                            last = mm(ps[:, 2 * (t % 2) + h, :], cat[:, k, t * P:(t + 1) * P], wout[:, k, h * W:(h + 1) * W],
                                      start=k == 0, stop=k == KD - 1)
                        if h == 0 and t == 0:
                            squares()
                        if h == 0 and t >= 2:
                            logits(t - 2)
                else:
                    logits(t - 2)
                    pe.wait_ge(s_cat, 1)
                    for k in range(KD):
                        for h in range(2):
                            last = mm(ps[h * TS:(h + 1) * TS, 2 * (t % 2) + h, :], cat[:, k, t * P:T], wout[:, k, h * W:(h + 1) * W],
                                      start=k == 0, stop=k == KD - 1)
                last.then_inc(s_op, 1)
                if t:
                    x1_transpose(t - 1)
            logits(NT - 2)
            x1_transpose(NT - 1)
            logits(NT - 1)

            pe.wait_ge(s_oh, 1)
            mm(ps[:, 0, 0:NT * NE], tri16, counts, start=True, stop=True)
            mm(ps[:, 1, 0:NT * NE], ones16, counts, start=True, stop=True).then_inc(s_rk, 1)
            for n in range(2 * NT):
                pe.wait_ge(s_ab, n // NT + 1)
                mm(ps[:, 2, 0:NPAIR], posoh[:, n, :], pairlo[:, n, :], start=n == 0, stop=False)
                last = mm(ps[:, 2, 0:NPAIR], posoh[:, n, :], pairhi[:, n, :], start=False, stop=n == 2 * NT - 1)
            last.then_inc(s_tab, 1)

            def rows_transpose(r, slot):
                pe.wait_ge(s_gx[slot], 16 * r + 16)
                for half in range(2):
                    for kk in range(4):
                        k = 4 * half + kk
                        last = tr(ps[:, 2 + half, kk * P:(kk + 1) * P], xg[slot].rearrange("p (c k) -> p k c", k=KD)[:, k, :], ident)
                    last.then_inc(s_xt, 1)

            rows_transpose(0, 0)

            def pair(r, slot):
                j = RING * r + slot
                pe.wait_ge(s_xa, j + 1)
                pe.wait_ge(s_xd, j + 1)
                for u in range(2):
                    pe.wait_ge(s_wgu[slot][u], 32 * r + 32)
                    gu = area((2 * slot + u) * TILEW, 2, KD, FE)
                    pe.wait_ge(s_info, 1)
                    for k in range(KD):
                        for fh in range(2):
                            last = mm(ps[fh * 64:fh * 64 + 64, u, 0:256], xTm[:, k, u * CAP:(u + 1) * CAP], gu[:, :, k, fh * P:(fh + 1) * P],
                                      start=k == 0, stop=k == KD - 1)
                    last.then_inc(s_gu[u], 1)

                def hidden_transpose(u):
                    pe.wait_ge(s_h[u], j + 1)
                    tr(ps[:, 4, u * P:(u + 1) * P], hid[u], ident).then_inc(s_ht[u], 1)

                def down(u):
                    pe.wait_ge(s_hc[u], j + 1)
                    pe.wait_ge(s_wd[slot][u], 16 * r + 16)
                    dn = area((2 * slot + u) * TILEW + GUW, 2, D)
                    if not (isinstance(j, int) and j == 0):
                        pe.wait_ge(s_yc[u], j)
                    pe.wait_ge(s_info, 1)
                    for fh in range(2):
                        for dh in range(2):
                            last = mm(ps[dh * 64:dh * 64 + 64, 5 + u, :], hT[u][:, fh * CAP:(fh + 1) * CAP], dn[:, fh, dh * W:(dh + 1) * W],
                                      start=fh == 0, stop=fh == 1)
                    last.then_inc(s_y[u], 1)

                hidden_transpose(0)
                rows_transpose(r if slot < RING - 1 else r + 1, (slot + 1) % RING)
                down(0)
                hidden_transpose(1)
                down(1)

            for slot in range(RING):
                pair(0, slot)
            full, rest = moe_size(pe)
            with pe.Fori(1, full) as r:
                for slot in range(RING):
                    pair(r, slot)
            for slot in range(RING - 1):
                with pe.If(rest[slot] > 0):
                    pair(full_rounds(pe, slot + 1), slot)

            pe.wait_ge(s_diag, 1)
            for t in range(DVE_SUMS, NT):
                r = rows(t)
                pe.wait_ge(s_yg[t], 32)
                if t >= DVE_SUMS + 2:
                    pe.wait_ge(s_mv2, t - 1)
                for h in range(2):
                    for k in range(2):
                        last = mm(ps[0:r, 2 * (t % 2) + h, :], diag[0:r, k * NT + t, 0:r], yg[0:r, t, k, h * W:(h + 1) * W], start=k == 0, stop=k == 1)
                last.then_inc(s_yw, 1)

        @block.scalar
        def _(act):
            a = nc.scalar
            def x_half(t, half, dst, src_sem, count, done):
                act.wait_ge(src_sem, count)
                a.copy(dst[:, 4 * half:4 * half + 4, t * P:t * P + rows(t)],
                       ps[:, 4 + half, :].rearrange("p (k c) -> p k c", k=4)[:, :, 0:rows(t)]).then_inc(done, 1)

            for t in range(NT):
                x_half(t, 1, xT, s_xtp, 2 * t + 2, s_xe[1])
            act.wait_ge(s_win[1], 16)
            act.wait_ge(s_zero, 1)
            for n in range(PAIR0, PAIRS):
                act.dma_start(y_slots[n * P:(n + 1) * P, :], zeros).then_inc(s_fill, 16)
            act.dma_start(ptab[0:1, 0:NB * NPG], A["page_table"].rearrange("b n -> (b n)").unsqueeze(0)).then_inc(s_pt, 16)
            for n, name in enumerate(("lambda_q1", "lambda_k1", "lambda_q2", "lambda_k2")):
                act.dma_start(lamv[:, n, :], A[name][0:1, :].to_broadcast([P, BLK])).then_inc(s_ln1, 16)
            act.dma_start(g08, A["subln_g"][0].unsqueeze(1)).then_inc(s_ln1, 16)
            act.dma_start(lng, A["ln1_g"][0:1, :].to_broadcast([P, D])).then_inc(s_ln1, 16)
            act.dma_start(lnb, A["ln1_b"][0:1, :].to_broadcast([P, D])).then_inc(s_ln1, 16)
            act.wait_ge(s_le, 1)
            a.activation(lex, lex, ACT.Exp).then_inc(s_lex, 1)
            unit = 4
            for m in range(4):
                act.wait_ge(s_pj, unit + m + 1)
                b = 2 * ((unit + m) % 2)
                for h in range(2):
                    a.activation(cat[:, 4 + m, h * HALF:(h + 1) * HALF], ps[:, b + h, 0:HALF], ACT.Gelu_apprx_tanh).then_inc(s_pev[(unit + m) % 2], 1)
            unit = 8
            act.wait_ge(s_prm, 1)
            for m in range(8):
                act.wait_ge(s_pj, unit + m + 1)
                b = 2 * ((unit + m) % 2)
                dst = (rg, ig)[m % 2]
                for h in range(2):
                    a.activation(dst[:, m // 2, h * HALF:(h + 1) * HALF], ps[:, b + h, 0:HALF], ACT.Sigmoid,
                                 bias=prm[:, m // 2, 5 + m % 2:6 + m % 2]).then_inc(s_pev[(unit + m) % 2], 1)
            unit = 16

            def q_unit(m):
                act.wait_ge(s_cst, 3)
                act.wait_ge(s_pj, unit + m + 1)
                b = 2 * ((unit + m) % 2)
                a.mul(qz[0:64, m, 0, 0:HALF], ps[0:64, b, 0:HALF], 0.125)
                a.mul(qz[0:64, m, 0, HALF:SEQ], ps[0:64, b + 1, 0:SEQ - HALF], 0.125)
                a.mul(qd[0:64, :, m, 0:SD], ps[0:64, b + 1, SEQ - HALF:HALF].rearrange("p (b s) -> p b s", s=SD), 0.125).then_inc(s_pev[(unit + m) % 2], 1)

            act.wait_ge(s_lam, 1)
            for n in range(2):
                act.wait_ge(s_pev[n], 16)
            for t in range(4):
                q_unit(t)
                a.activation(th[:, t, :], rg[:, t, :], ACT.Tanh, scale=cl[:, t, 0:1]).then_inc(s_th, 1)
                act.wait_ge(s_th, 2 * t + 1)
                a.activation(rg[:, t, :], rg[:, t, :], ACT.Exp, scale=cl[:, t, 0:1]).then_inc(s_th, 1)
            unit = 20
            for m in range(4):
                act.wait_ge(s_pj, unit + m + 1)
                b = 2 * ((unit + m) % 2)
                for h in range(2):
                    a.copy(kTn[:, m, h * HALF:(h + 1) * HALF], ps[:, b + h, 0:HALF]).then_inc(s_pev[(unit + m) % 2], 1)
                if m == 1:
                    act.wait_ge(s_m2, 1)
                    a.activation(th, th, ACT.Sqrt).then_inc(s_mult, 1)
            unit = 24
            for t in range(NT):
                act.wait_ge(s_cst, 3)
                act.wait_ge(s_pj, unit + t + 1)
                b = 2 * ((unit + t) % 2)
                if t < NT - 1:
                    a.copy(vn[:, t, :], ps[:, b, :]).then_inc(s_pev[(unit + t) % 2], 2)
                else:
                    for h in range(2):
                        a.copy(vn[0:TS, t, h * W // 2:(h + 1) * W // 2], ps[h * TS:(h + 1) * TS, b + h, 0:W // 2]).then_inc(s_pev[(unit + t) % 2], 1)
                act.wait_ge(s_kt, t + 1)
                if t >= 2:
                    act.wait_ge(s_kout[t % 2], 16 * (t // 2))
                a.copy(kstage[0:rows(t), t % 2, :], ps[0:rows(t), 4 + t % 2, :]).then_inc(s_kc, 1)
            act.wait_ge(s_dc, 1)
            a.activation(sc[:, 4:6], sc[:, 0:2], ACT.Exp).then_inc(s_lexp, 1)

            act.wait_ge(s_endp, 1)
            a.copy(ends_out[0:36, :], ps[0:36, 6, :]).then_inc(s_endc, 1)

            def exps(n):
                i, heads = STEPS[n]
                w = (i + 1) * P
                act.wait_ge(s_mxp, n + 1)
                if n >= 2:
                    act.wait_ge(s_w, n - 1)
                for m in range(2):
                    for j in range(len(heads)):
                        last = a.activation(pexp[n % 2][:, m, j * w:(j + 1) * w], ps[:, 2 * (n % 2) + m, j * w:(j + 1) * w], ACT.Exp,
                                            bias=mx[:, n % 2, m, j:j + 1], accum_out=sm[:, n % 2, m, j:j + 1])
                last.then_inc(s_exp, 1)

            def o_out(i):
                act.wait_ge(s_ot, i + 1)
                a.activation(cat[:, 0:NH, i * P:(i + 1) * P], ps[:, 7, :].rearrange("p (h c) -> p h c", h=NH), ACT.Copy,
                             scale=g08[:, 0:1]).then_inc(s_oe, 1)

            def weights_out(n):
                i, heads = STEPS[n]
                w = len(heads) * (i + 1) * P
                act.wait_ge(s_wt, n + 1)
                if n >= 2:
                    act.wait_ge(s_pvp, n - 1)
                a.copy(wT[n % 2][:, 0:w], ps[:, 4 + n % 2, 0:w]).then_inc(s_wc, 1)

            exps(0)
            exps(1)
            weights_out(0)
            exps(2)
            for n in range(len(STEPS)):
                if n + 1 < len(STEPS):
                    weights_out(n + 1)
                if tile_ended(n, 0) is not None:
                    i = tile_ended(n, 0)
                    act.wait_ge(s_pvp, n + 1)
                    if i == 1:
                        act.wait_ge(s_kout[0], 16 * 3)
                    if i >= 2:
                        act.wait_ge(s_ot, i - 1)
                    a.copy(osb[i % 2].rearrange("p h c -> p (h c)"), ps[:, 6, :]).then_inc(s_oc, 1)
                if n + 3 < len(STEPS):
                    exps(n + 3)
                if tile_ended(n, 3) is not None:
                    o_out(tile_ended(n, 3))

            act.wait_ge(s_sp, len(STEPS))
            act.dma_start(wr[:, :, 0:NG], A["w_group_router"][0].rearrange("(k p) g -> p k g", p=P)).then_inc(s_rt, 16)
            act.dma_start(wr[:, :, NG:NG + NE], A["w_expert_router"][0].rearrange("(k p) g -> p k g", p=P)).then_inc(s_rt, 16)
            act.dma_start(rbias[:, 0:NG], A["b_group_router"][0:1, :].to_broadcast([P, NG])).then_inc(s_rt, 16)
            act.dma_start(rbias[:, NG:NG + NE], A["b_expert_router"][0:1, :].to_broadcast([P, NE])).then_inc(s_rt, 16)

            def probs(b, grp):
                act.wait_ge(s_ptp, 3 * b + grp + 1)
                act.wait_ge(s_cst, 3)
                k0, k1 = ((0, 4), None, (8, 9))[grp]
                a.copy(pT[:, k0:k1, :], ps[:, 5, 0:(k1 - k0) * P].rearrange("p (k c) -> p k c", c=P)).then_inc(s_pta, 1)

            def keys_out(b, g):
                act.wait_ge(s_ktp[0], 4 * b + g // 2 + 1)
                act.wait_ge(s_sc, b)
                a.copy(kT[:, :, g * P:(g + 1) * P], ps[:, 3, :].rearrange("p (h c) -> p h c", h=NH)).then_inc(s_ktc[0], 1)

            def sample(b, u, last=False):
                if not last:
                    keys_out(b + 1, 0)
                act.wait_ge(s_mxs, b + 1)
                act.wait_ge(s_cst, 3)
                a.activation(pes[u].rearrange("p (c k) j -> p c (k j)", c=3), ps[:, 0:3, 0:384], ACT.Exp,
                             bias=coef[:, u:u + 1], accum_out=coef[:, 2 + u:3 + u]).then_inc(s_exs, 1)
                if not last:
                    keys_out(b + 1, 2)
                probs(b, 0)
                if not last:
                    keys_out(b + 1, 4)
                probs(b, 2)
                if not last:
                    keys_out(b + 1, 6)

            for g in range(0, NPG, 2):
                keys_out(0, g)
            o_out(NT - 2)
            sample(0, 0)
            with act.Fori(0, NB // 2 - 1) as jb:
                sample(2 * jb + 1, 1)
                sample(2 * jb + 2, 0)
            sample(NB - 1, 1, last=True)
            act.wait_ge(s_sq, 2)
            a.activation(oTr, oTr, ACT.Sqrt).then_inc(s_srs, 1)

            def x1_half(t):
                x_half(t, 1, x1T, s_x1t, 2 * t + 2, s_x1e[1])

            for t in range(1, NT):
                x1_half(t - 1)
                act.dma_start(x1_dram[(t - 1) * P:t * P, :], x[:, t - 1, :]).then_inc(s_x1d, 16)
            act.wait_ge(s_x1, NT)
            act.dma_start(x1_dram[SEQ:T, :], x[0:TS, NT - 1, :]).then_inc(s_x1d, 16)
            x1_half(NT - 1)
            act.dma_start(lng, A["ln2_g"][0:1, :].to_broadcast([P, D])).then_inc(s_ln2, 16)
            act.dma_start(lnb, A["ln2_b"][0:1, :].to_broadcast([P, D])).then_inc(s_ln2, 16)
            act.wait_ge(s_re, 1)
            a.activation(rexp, rexp, ACT.Exp).then_inc(s_rx, 1)

            act.wait_ge(s_info, 1)
            full, rest = moe_size(act)

            def x_rows(j):
                act.wait_ge(s_xt, 2 * j + 1)
                act.wait_ge(s_info, 1)
                a.copy(xTm[:, 0:4, :].rearrange("p k c -> p (k c)"), ps[:, 2, :]).then_inc(s_xa, 1)

            x_rows(0)

            def pair(r, slot):
                j = RING * r + slot
                for u in range(2):
                    act.wait_ge(s_gu[u], j + 1)
                    a.activation(sg[u], ps[:, u, 0:P], ACT.Silu).then_inc(s_sg[u], 1)
                x_rows(j + 1)
                for u in range(2):
                    act.wait_ge(s_y[u], j + 1)
                    if not isinstance(r, int):
                        act.wait_ge(s_yd[slot], 64 * r)
                    a.copy(ysb[slot][u], ps[:, 5 + u, :]).then_inc(s_yc[u], 1)
                    act.wait_ge(s_yc[u], j + 1)
                    for dh in range(2):
                        act.dma_start(y_slots[bass.ds((2 * j + u) * CAP, CAP), dh * W:(dh + 1) * W], ysb[slot][u][dh * 64:dh * 64 + 64, :]).then_inc(s_yd[slot], 16)

            for slot in range(RING):
                pair(0, slot)
            with act.Fori(1, full) as r:
                for slot in range(RING):
                    pair(r, slot)
            for slot in range(RING - 1):
                with act.If(rest[slot] > 0):
                    pair(full_rounds(act, slot + 1), slot)

            for t in range(NT - 1):
                r = rows(t)
                act.wait_ge(s_rstd2, t + 1)
                act.wait_ge(s_mvn, t + 1)
                a.activation(x[0:r, t, :], x[0:r, t, :], ACT.Identity, scale=pw[0:r, t:t + 1], bias=mv[0:r, t, 0:1]).then_inc(s_nrm2, 1)

        @block.vector
        def _(dve):
            v = nc.vector
            cnt = [0]

            def link(ins):
                cnt[0] += 1
                ins.then_inc(s_ch, 1)
                dve.wait_ge(s_ch, cnt[0])

            def x_half(t, dst, src_sem, count, done):
                dve.wait_ge(src_sem, count)
                v.tensor_copy(dst[:, 0:4, t * P:t * P + rows(t)],
                              ps[:, 4, :].rearrange("p (k c) -> p k c", k=4)[:, :, 0:rows(t)]).then_inc(done, 1)

            for t in range(NT):
                x_half(t, xT, s_xtp, 2 * t + 1, s_xe[0])
            dve.wait_ge(s_rows, 1)
            v.tensor_copy(prm, ps[:, 6, 0:160].rearrange("p (t c) -> p t c", c=40)).then_inc(s_prm, 1)
            dve.wait_ge(s_prm, 1)
            dve.wait_ge(s_cst, 3)
            link(v.tensor_copy(xl[:, :, XSEG:].rearrange("p t (b c) -> p t b c", c=SSEG)[:, :, :, 0:3],
                               prm[:, :, 16:40].rearrange("p t (b j) -> p t b j", j=3)))
            y, e = cl[:, :, 0:1], cl[:, :, 1:2]
            s, s2 = cl[:, :, 2:3], cl[:, :, 3:4]
            link(v.tensor_scalar(y, prm[:, :, 7:8], -1.0, None, ALU.mult))
            link(v.tensor_tensor(e, y, prm[:, :, 7:8], ALU.min))
            v.tensor_copy(lex, e).then_inc(s_le, 1)
            for m in range(4):
                dve.wait_ge(s_pj, m + 1)
                b = 2 * (m % 2)
                v.tensor_copy(xl[:, m, 3:3 + HALF], ps[:, b, 0:HALF])
                v.tensor_copy(xl[:, m, 3 + HALF:XSEG], ps[:, b + 1, 0:SEQ - HALF]).then_inc(s_pev[m % 2], 1)
                v.tensor_copy(xl[:, m, XSEG:].rearrange("p (b c) -> p b c", c=SSEG)[:, :, 3:],
                              ps[:, b + 1, SEQ - HALF:HALF].rearrange("p (b s) -> p b s", s=SD)).then_inc(s_pev[m % 2], 1)
                dve.wait_ge(s_pev[m % 2], 2 * (m // 2) + 2)
                xs = xl[:, m, XSEG:].rearrange("p (b c) -> p b c", c=SSEG)
                op, osmp = xc[:, m, 0:SEQ], xc[:, m, SEQ:T].rearrange("p (b s) -> p b s", s=SD)
                v.tensor_scalar(op, xl[:, m, 0:SEQ], prm[:, m, 0:1], prm[:, m, 4:5], ALU.mult, ALU.add)
                link(v.tensor_scalar(osmp, xs[:, :, 0:SD], prm[:, m, 0:1], prm[:, m, 4:5], ALU.mult, ALU.add))
                for j in range(1, 4):
                    v.scalar_tensor_tensor(out=op, in0=xl[:, m, j:j + SEQ], scalar=prm[:, m, j:j + 1], in1=op, op0=ALU.mult, op1=ALU.add)
                    last = v.scalar_tensor_tensor(out=osmp, in0=xs[:, :, j:j + SD], scalar=prm[:, m, j:j + 1], in1=osmp, op0=ALU.mult, op1=ALU.add)
                    link(last)
                dve.sem_inc(s_xc, 1)
            dve.wait_ge(s_lex, 1)
            link(v.tensor_scalar(s2, lex, 2.0, None, ALU.add))
            link(v.reciprocal(s2, s2))
            link(v.tensor_tensor(s, lex, s2, ALU.mult))
            link(v.tensor_tensor(s2, s, s, ALU.mult))
            link(v.tensor_scalar(e, s2, 1.0 / 15, 1.0 / 13, ALU.mult, ALU.add))
            for n in (11, 9, 7, 5, 3, 1):
                link(v.tensor_tensor(e, e, s2, ALU.mult))
                link(v.tensor_scalar(e, e, 1.0 / n, None, ALU.add))
            link(v.tensor_tensor(e, e, s, ALU.mult))
            link(v.tensor_scalar(y, y, 0.0, -LRU_C, ALU.max, ALU.mult))
            link(v.scalar_tensor_tensor(out=y, in0=e, scalar=-2.0 * LRU_C, in1=y, op0=ALU.mult, op1=ALU.add))
            dve.sem_inc(s_lam, 1)

            dve.wait_ge(s_ln1, 16 * 7)
            link(v.tensor_tensor(lamv[:, 0, :], lamv[:, 0, :], lamv[:, 1, :], ALU.mult))
            link(v.tensor_tensor(lamv[:, 2, :], lamv[:, 2, :], lamv[:, 3, :], ALU.mult))
            link(v.tensor_reduce(sc[:, 0:1], lamv[:, 0, :], AX.X, ALU.add))
            link(v.tensor_reduce(sc[:, 1:2], lamv[:, 2, :], AX.X, ALU.add))
            link(v.tensor_scalar(g08, g08, 1.0 - LAM_INIT, None, ALU.mult))
            sel0, sel1 = sel01
            link(v.tensor_copy(iotf, ioti))
            link(v.tensor_scalar(parti, parti, SD - 1, None, ALU.bitwise_and))
            link(v.tensor_copy(partf, parti))
            link(v.tensor_scalar(bigm, iotf, partf[:, 0:1], None, ALU.is_le))
            link(v.scalar_tensor_tensor(out=bigm, in0=iotf, scalar=0.0, in1=bigm, op0=ALU.is_ge, op1=ALU.mult))
            link(v.tensor_scalar(bigm, bigm, 1.0, -NEG, ALU.subtract, ALU.mult))
            link(v.tensor_tensor(sel, sel0, sel1, ALU.add))
            link(v.tensor_reduce(sc[:, 6:7], sel0, AX.X, ALU.add))
            link(v.tensor_reduce(sc[:, 7:8], sel1, AX.X, ALU.add))
            dve.sem_inc(s_dc, 1)

            unit = 16
            for m in range(4):
                dve.wait_ge(s_pj, unit + m + 1)
                b = 2 * ((unit + m) % 2)
                v.tensor_scalar(qz[64:P, m, 1, 0:HALF], ps[64:P, b, 0:HALF], 0.125, None, ALU.mult)
                v.tensor_scalar(qz[64:P, m, 1, HALF:SEQ], ps[64:P, b + 1, 0:SEQ - HALF], 0.125, None, ALU.mult)
                v.tensor_scalar(qd[64:P, :, m, SD:2 * SD], ps[64:P, b + 1, SEQ - HALF:HALF].rearrange("p (b s) -> p b s", s=SD),
                                0.125, None, ALU.mult).then_inc(s_pev[(unit + m) % 2], 1)
            dve.wait_ge(s_th, 8)
            dve.wait_ge(s_fill, 16 * (PAIRS - PAIR0))
            link(v.tensor_scalar(hh, th, -1.0, 1.0, ALU.mult, ALU.add))
            link(v.reciprocal(hh, hh))
            link(v.scalar_tensor_tensor(out=th, in0=th, scalar=-2.0, in1=hh, op0=ALU.mult, op1=ALU.mult))
            link(v.tensor_scalar(th, th, 0.0, None, ALU.max))
            dve.sem_inc(s_m2, 1)
            link(v.tensor_tensor(ig, ig, xc, ALU.mult))
            dve.wait_ge(s_mult, 1)
            link(v.tensor_tensor(ig, ig, th, ALU.mult))
            a0 = rg[:, :, SEQ:T].rearrange("p t (b s) -> p t b s", s=SD)[:, :, :, 0]
            u0 = ig[:, :, SEQ:T].rearrange("p t (b s) -> p t b s", s=SD)[:, :, :, 0]
            link(v.tensor_tensor(th[:, :, 0:NB], a0, prm[:, :, 8:16], ALU.mult))
            link(v.tensor_tensor(u0, u0, th[:, :, 0:NB], ALU.add))
            link(v.tensor_scalar(a0, a0, 0.0, None, ALU.mult))
            for t in range(4):
                link(v.tensor_tensor_scan(hh[:, t, :], rg[:, t, :], ig[:, t, :], 0.0, ALU.mult, ALU.add))
            link(v.tensor_tensor(cat[:, 4:8, :], cat[:, 4:8, :], hh, ALU.mult))
            v.tensor_copy(ends[:, :, 0:1], hh[:, :, SEQ - 1:SEQ])
            v.tensor_copy(ends[:, :, 1:9], hh[:, :, SEQ:T].rearrange("p t (b s) -> p t b s", s=SD)[:, :, :, SD - 1])
            v.tensor_copy(ends[:, :, 9:12], xl[:, :, XSEG - 3:XSEG])
            link(v.tensor_copy(ends[:, :, 12:36].rearrange("p t (b j) -> p t b j", j=3),
                               xl[:, :, XSEG:].rearrange("p t (b c) -> p t b c", c=SSEG)[:, :, :, SD:SSEG]))
            dve.sem_inc(s_ends, 1)
            dve.wait_ge(s_lexp, 1)
            link(v.tensor_tensor(sc[:, 8:9], sc[:, 5:6], sc[:, 4:5], ALU.subtract))
            link(v.tensor_scalar(sc[:, 8:9], sc[:, 8:9], -LAM_INIT, None, ALU.add))
            link(v.scalar_tensor_tensor(out=sc[:, 9:10], in0=sc[:, 7:8], scalar=sc[:, 8:9], in1=sc[:, 6:7], op0=ALU.mult, op1=ALU.add))

            def maxima(n):
                i, heads = STEPS[n]
                w = len(heads) * (i + 1) * P
                dve.wait_ge(s_sp, n + 1)
                sps = ps[:, 2 * (n % 2):2 * (n % 2) + 2, 0:w].rearrange("p m (h c) -> p m h c", h=len(heads))
                diagonal = sps[:, :, :, i * P:]
                link(v.tensor_tensor(diagonal, diagonal, dmask.unsqueeze(1).unsqueeze(1).broadcast_to([P, 2, len(heads), P]), ALU.add))
                link(v.tensor_reduce(mx[:, n % 2, :, 0:len(heads)], sps, AX.X, ALU.max, negate=True))
                dve.sem_inc(s_mxp, 1)

            def weights_(n):
                i, heads = STEPS[n]
                nh, w = len(heads), (i + 1) * P
                dve.wait_ge(s_exp, n + 1)
                if n >= 2:
                    dve.wait_ge(s_wt, n - 1)
                r, wd_, pe_ = rc[:, n % 2, :, 0:nh], wdiff[n % 2], pexp[n % 2]
                link(v.reciprocal(r, sm[:, n % 2, :, 0:nh]))
                link(v.tensor_scalar(r[:, 1, :], r[:, 1, :], sc[:, 8:9], None, ALU.mult))
                for j in range(nh):
                    last = v.tensor_scalar(wd_[:, j * w:(j + 1) * w], pe_[:, 0, j * w:(j + 1) * w], r[:, 0, j:j + 1], None, ALU.mult)
                link(last)
                for j in range(nh):
                    last = v.scalar_tensor_tensor(out=wd_[:, j * w:(j + 1) * w], in0=pe_[:, 1, j * w:(j + 1) * w], scalar=r[:, 1, j:j + 1],
                                                  in1=wd_[:, j * w:(j + 1) * w], op0=ALU.mult, op1=ALU.add)
                last.then_inc(s_w, 1)

            def squares(i):
                if i == 0:
                    dve.wait_ge(s_out, 16 * 6)
                dve.wait_ge(s_oc, i + 1)
                link(v.tensor_tensor(osq, osb[i % 2], osb[i % 2], ALU.mult))
                link(v.tensor_reduce(ss, osq, AX.X, ALU.add))
                v.tensor_scalar(ss, ss, 1.0 / P, EPS, ALU.mult, ALU.add).then_inc(s_var, 1)

            def norm(i):
                dve.wait_ge(s_rs, i + 1)
                v.tensor_tensor(osb[i % 2], osb[i % 2], ss.unsqueeze(2).broadcast_to([P, NH, P]), ALU.mult).then_inc(s_on, 1)

            maxima(0)
            maxima(1)
            weights_(0)
            maxima(2)
            weights_(1)
            for n in range(len(STEPS)):
                if n + 3 < len(STEPS):
                    maxima(n + 3)
                if n + 2 < len(STEPS):
                    weights_(n + 2)
                if tile_ended(n, 1) is not None:
                    squares(tile_ended(n, 1))
                if tile_ended(n, 2) is not None:
                    norm(tile_ended(n, 2))
            squares(NT - 2)

            dve.wait_ge(s_pvp, len(STEPS))
            link(v.tensor_copy(kT[:, :, PAST:PAST + TS], kTn[:, :, SEQ:T]))
            link(v.memset(kT[:, :, PAST + TS:], 0.0))
            dve.sem_inc(s_dc, 1)
            step = [0]
            PER = 2

            def chain(b, ins):
                step[0] += 1
                ins.then_inc(s_sch, 1)
                dve.wait_ge(s_sch, PER * b + (step[0] - 1) % PER + 1)

            def keys_out(b, g):
                dve.wait_ge(s_ktp[1], 4 * b + g // 2 + 1)
                dve.wait_ge(s_sc, b)
                v.tensor_copy(kT[:, :, g * P:(g + 1) * P], ps[:, 4, :].rearrange("p (h c) -> p h c", h=NH)).then_inc(s_ktc[1], 1)

            def combined_out(b):
                dve.wait_ge(s_cmb, b + 1)
                dve.wait_ge(s_cst, 3)
                v.tensor_copy(arena[:, bass.ds(A_STG + W + 32 * b, 32)], ps[:, 7, 256:288]).then_inc(s_oct, 1)

            def sample(b, u, first=False, last=False):
                dve.wait_ge(s_sc, b + 1)
                dve.wait_ge(s_cst, 3)
                new = ps[:, 2, 256:384]
                v.tensor_tensor(new, new, bigm[:, bass.ds(56 - 8 * b, P)], ALU.add).then_inc(s_msk, 1)
                dve.wait_ge(s_msk, b + 1)
                dve.wait_ge(s_cst, 3)
                v.tensor_reduce(coef[:, u:u + 1], ps[:, 0:3, 0:384], AX.XY, ALU.max, negate=True).then_inc(s_mxs, 1)
                if not last:
                    keys_out(b + 1, 1)
                if not first:
                    combined_out(b - 1)
                if not last:
                    keys_out(b + 1, 3)
                dve.wait_ge(s_ptp, 3 * b + 2)
                dve.wait_ge(s_cst, 3)
                v.tensor_copy(pT[:, 4:8, :], ps[:, 6, :].rearrange("p (k c) -> p k c", c=P)).then_inc(s_ptd, 1)
                if not last:
                    keys_out(b + 1, 5)
                dve.wait_ge(s_exs, b + 1)
                chain(b, v.reciprocal(sc[:, 10 + u:11 + u], coef[:, 2 + u:3 + u]))
                chain(b, v.tensor_tensor(sc[:, 10 + u:11 + u], sc[:, 10 + u:11 + u], sc[:, 9:10], ALU.mult))
                if not last:
                    keys_out(b + 1, 7)
                dve.wait_ge(s_pvs, b + 1)
                dve.wait_ge(s_cst, 3)
                v.tensor_scalar(osm[u], ps[:, 7, 0:P], sc[:, 10 + u:11 + u], None, ALU.mult).then_inc(s_os, 1)

            for g in range(1, NPG, 2):
                keys_out(0, g)
                if g == 1:
                    norm(NT - 2)
            sample(0, 0, first=True)
            with dve.Fori(0, NB // 2 - 1) as jb:
                sample(2 * jb + 1, 1)
                sample(2 * jb + 2, 0)
            sample(NB - 1, 1, last=True)
            combined_out(NB - 1)
            dve.wait_ge(s_oct, NB)
            v.tensor_tensor(oTq, oTs, oTs, ALU.mult).then_inc(s_sq, 1)
            dve.wait_ge(s_sqm, 1)
            link(v.tensor_scalar(oTr.rearrange("p b c -> p (b c)"), ps[:, 6, 0:NB * 32], 1.0 / P, EPS, ALU.mult, ALU.add))
            v.reciprocal(oTr, oTr).then_inc(s_sq, 1)
            dve.wait_ge(s_srs, 1)
            link(v.tensor_tensor(oTs, oTs, oTr, ALU.mult))
            dve.wait_ge(s_oe, NT - 1)
            link(v.tensor_scalar(cat[:, 0:NH, SEQ:T].rearrange("p h (b s) -> p b h s", s=SD),
                                 oTs.rearrange("p b (h s) -> p b h s", s=SD), g08[:, 0:1], None, ALU.mult))
            dve.sem_inc(s_cat, 1)

            def stats(t, done):
                r = rows(t)
                v.bn_stats(st[0:r, 0:6], x[0:r, t, 0:512])
                link(v.bn_stats(st[0:r, 6:12], x[0:r, t, 512:D]))
                link(v.bn_aggr(mv[0:r, t, :], st[0:r, :]))
                v.tensor_scalar(pw[0:r, t:t + 1], mv[0:r, t, 1:2], EPS, None, ALU.add).then_inc(done, 1)

            def neg_mean(t, ready, n):
                r = rows(t)
                dve.wait_ge(ready, n)
                v.scalar_tensor_tensor(out=mv[0:r, t, 0:1], in0=mv[0:r, t, 0:1], scalar=-1.0, in1=pw[0:r, t:t + 1], op0=ALU.mult, op1=ALU.mult).then_inc(s_mvn, 1)

            dve.wait_ge(s_lc, 5)
            link(v.tensor_copy(io128f, io128i))
            link(v.tensor_copy(tokf, toki))
            link(v.tensor_scalar(valid, tokf, float(T), None, ALU.is_lt))
            link(v.tensor_tensor(tokf, tokf, valid, ALU.mult))
            link(v.tensor_scalar(toklo, valid, tokf[:, 0:1], None, ALU.mult))
            link(v.tensor_tensor(tokhi, tokf, toklo, ALU.subtract))
            v.tensor_copy(ones16, ones)
            v.tensor_copy(tri16, tri)
            link(v.tensor_scalar(capt, io128f[:, 0:MOREQ], 1.0, float(CAP), ALU.add, ALU.mult))
            link(v.tensor_scalar(pairt, io128f[:, 0:NPAIR - 1], 1.0, float(P), ALU.add, ALU.mult))
            link(v.tensor_copy(info[:, I_TAB:I_TAB + NE - TAB0], io128f[:, TAB0:NE]))
            link(v.memset(L, 0.0))
            link(v.memset(pw, 1.0))
            for t in range(NT):
                r = rows(t)
                dve.wait_ge(s_op, t + 1)
                if t < NT - 1:
                    link(v.scalar_tensor_tensor(out=x[0:r, t, :], in0=x[0:r, t, :], scalar=ALPHA,
                                                in1=ps[0:r, 2 * (t % 2):2 * (t % 2) + 2, :].rearrange("p a b -> p (a b)"), op0=ALU.mult, op1=ALU.add))
                else:
                    for h in range(2):
                        xh = x[0:r, t, h * W:(h + 1) * W]
                        link(v.scalar_tensor_tensor(out=xh, in0=xh, scalar=ALPHA, in1=ps[h * TS:(h + 1) * TS, 2 * (t % 2) + h, :],
                                                    op0=ALU.mult, op1=ALU.add))
                dve.sem_inc(s_opr, 1)
                stats(t, s_mv)
                if t:
                    x_half(t - 1, x1T, s_x1t, 2 * (t - 1) + 1, s_x1e[0])
                xt = x[0:r, t, :]
                link(v.scalar_tensor_tensor(out=xt, in0=xt, scalar=mv[0:r, t, 0:1], in1=lng[0:r, :], op0=ALU.subtract, op1=ALU.mult))
                dve.wait_ge(s_rstd, t + 1)
                v.scalar_tensor_tensor(out=xt, in0=xt, scalar=pw[0:r, t:t + 1], in1=lnb[0:r, :], op0=ALU.mult, op1=ALU.add).then_inc(s_x1, 1)
            x_half(NT - 1, x1T, s_x1t, 2 * NT - 1, s_x1e[0])

            dve.wait_ge(s_lgt, NT)
            psl = ps[:, 6, 0:NT * 36].rearrange("p (t c) -> p t c", c=36)
            v.tensor_tensor(L[:, 0:NT - 1, :], psl[:, 0:NT - 1, :], rbias.unsqueeze(1).broadcast_to([P, NT - 1, 36]), ALU.add)
            link(v.tensor_tensor(L[0:TS, NT - 1, :], psl[0:TS, NT - 1, :], rbias[0:TS, :], ALU.add))
            def over(ap, m):
                return ap.unsqueeze(2).broadcast_to([P, ap.shape[1], m])

            def under(ap, n):
                return ap.unsqueeze(1).broadcast_to([P, n, ap.shape[1]])

            def first_max(src, n, out_max, onehot, tmp, first):
                link(v.tensor_reduce(out_max, src, AX.X, ALU.max))
                link(v.tensor_tensor(tmp, src, over(out_max, n), ALU.is_equal))
                link(v.tensor_scalar(tmp, tmp, -1000.0, None, ALU.mult))
                link(v.tensor_tensor(tmp, tmp, under(io128f[:, 0:n], NT), ALU.add))
                link(v.tensor_reduce(first, tmp, AX.X, ALU.min))
                link(v.tensor_tensor(onehot, tmp, over(first, n), ALU.is_equal))

            first_max(L[:, :, 0:NG], NG, gmax, goh, t8[:, :, 0:NG], gfirst)
            link(v.tensor_tensor(rexp[:, :, 0:NG], L[:, :, 0:NG], over(gmax, NG), ALU.subtract))
            el = L[:, :, NG:].rearrange("p t (g e) -> p t g e", g=NG)
            ing = ohs.rearrange("p t (g e) -> p t g e", g=NG)
            link(v.tensor_tensor(ing, el, goh.unsqueeze(3).broadcast_to([P, NT, NG, EPG]), ALU.mult))
            link(v.tensor_reduce(wi, ohs.rearrange("p t (g e) -> p t e g", g=NG), AX.X, ALU.add))
            first_max(wi, EPG, m1, oh1, t8, efirst[:, 0, :])
            link(v.scalar_tensor_tensor(out=wi, in0=oh1, scalar=-3e38, in1=wi, op0=ALU.mult, op1=ALU.add))
            first_max(wi, EPG, m2, oh2, t8, efirst[:, 1, :])
            link(v.tensor_tensor(rexp[:, :, NG], m2, m1, ALU.subtract))
            dve.sem_inc(s_re, 1)
            link(v.tensor_tensor(goh, goh, over(valid, NG), ALU.mult))
            for k, oh in enumerate((oh1, oh2)):
                link(v.tensor_tensor(ek[:, k * NT:(k + 1) * NT, :].rearrange("p t (g e) -> p t g e", g=NG),
                                     goh.unsqueeze(3).broadcast_to([P, NT, NG, EPG]),
                                     oh.unsqueeze(2).broadcast_to([P, NT, NG, EPG]), ALU.mult))
            link(v.tensor_tensor(counts.rearrange("p (t e) -> p t e", e=NE), ek[:, 0:NT, :], ek[:, NT:, :], ALU.add))
            dve.sem_inc(s_oh, 1)
            link(v.tensor_scalar(gfirst, gfirst, 1000.0, float(EPG), ALU.add, ALU.mult))
            link(v.scalar_tensor_tensor(out=re_.rearrange("p (k t) -> p k t", k=2), in0=efirst, scalar=1000.0,
                                        in1=gfirst.unsqueeze(1).broadcast_to([P, 2, NT]), op0=ALU.add, op1=ALU.add))
            dve.wait_ge(s_rk, 1)
            tot = ps[:, 1, 0:NT * NE].rearrange("p (t e) -> p t e", e=NE)
            link(v.tensor_copy(rank, ps[:, 0, 0:NT * NE].rearrange("p (t e) -> p t e", e=NE)))
            link(v.tensor_copy(run, tot[:, 0, :]))
            for t in range(1, NT):
                link(v.tensor_tensor(rank[:, t, :], rank[:, t, :], run, ALU.add))
                link(v.tensor_tensor(run, run, tot[:, t, :], ALU.add))
            full = cmp8.rearrange("p a b -> p (a b)")[:, 0:NE * MOREQ].rearrange("p (e n) -> p e n", n=MOREQ)
            link(v.tensor_tensor(full, over(run, MOREQ), under(capt, NE), ALU.is_gt))
            link(v.tensor_reduce(more, full, AX.X, ALU.add))
            link(v.tensor_scalar(run, run, 0.0, 1.0, ALU.mult, ALU.add))
            link(v.tensor_tensor_scan(upto, run, more, 0.0, ALU.mult, ALU.add))
            link(v.tensor_tensor(before, upto, more, ALU.subtract))
            tables = (rk, rank.unsqueeze(1).broadcast_to([P, 2, NT, NE])), \
                (rb, before.unsqueeze(1).unsqueeze(1).broadcast_to([P, 2, NT, NE]))
            for dst, table in tables:
                link(v.tensor_tensor(ekx.rearrange("p (k t) e -> p k t e", k=2), ek.rearrange("p (k t) e -> p k t e", k=2), table, ALU.mult))
                link(v.tensor_reduce(dst, ekx, AX.X, ALU.add))
            link(v.tensor_tensor(cmp8[:, :, 0:MOREQ], over(rk, MOREQ), under(capt, 2 * NT), ALU.is_ge))
            link(v.tensor_reduce(rf, cmp8[:, :, 0:MOREQ], AX.X, ALU.add))
            link(v.tensor_tensor(rb, rb, rf, ALU.add))
            link(v.scalar_tensor_tensor(out=rb, in0=rb, scalar=float(NE - 1), in1=re_, op0=ALU.add, op1=ALU.subtract))
            link(v.scalar_tensor_tensor(out=rb, in0=rf, scalar=1.0, in1=rb, op0=ALU.is_ge, op1=ALU.mult))
            link(v.tensor_tensor(rb, rb, re_, ALU.add))
            link(v.tensor_tensor(rb, rb, rf, ALU.subtract))
            link(v.scalar_tensor_tensor(out=rs, in0=rb, scalar=float(CAP), in1=rk, op0=ALU.mult, op1=ALU.add))
            link(v.tensor_tensor(cmp8[:, :, 0:NPAIR - 1], over(rs, NPAIR - 1), under(pairt, 2 * NT), ALU.is_ge))
            link(v.tensor_reduce(rf, cmp8[:, :, 0:NPAIR - 1], AX.X, ALU.add))
            link(v.scalar_tensor_tensor(out=rb, in0=rf, scalar=-float(P), in1=rs, op0=ALU.mult, op1=ALU.add))
            link(v.tensor_tensor(pairoh, under(io128f[:, 0:NPAIR], 2 * NT), over(rf, NPAIR), ALU.is_equal))
            for dst, tok in ((pairlo, toklo), (pairhi, tokhi)):
                link(v.tensor_tensor(dst.rearrange("p (k t) c -> p k t c", k=2), pairoh.rearrange("p (k t) c -> p k t c", k=2),
                                     tok.unsqueeze(1).unsqueeze(3).broadcast_to([P, 2, NT, NPAIR]), ALU.mult))
            for k in range(2):
                v.tensor_tensor(posoh[:, k * NT:(k + 1) * NT, :], under(io128f, NT), over(rb[:, k * NT:(k + 1) * NT], P), ALU.is_equal).then_inc(s_ab, 1)
            dve.wait_ge(s_tab, 1)
            v.tensor_copy(idx, ps[:, 2, 0:NPAIR]).then_inc(s_idx, 1)
            dve.wait_ge(s_rx, 1)
            link(v.tensor_reduce(m1, rexp[:, :, 0:NG], AX.X, ALU.add))
            link(v.tensor_scalar(m2, rexp[:, :, NG], 1.0, None, ALU.add))
            link(v.tensor_tensor(m1, m1, m2, ALU.mult))
            link(v.reciprocal(wgt[:, 0, :], m1))
            link(v.tensor_tensor(wgt[:, 1, :], wgt[:, 0, :], rexp[:, :, NG], ALU.mult))
            link(v.tensor_copy(yidx.rearrange("p k t -> p (k t)"), rs))
            size = cmp8.rearrange("p a b -> p (a b)")
            evens, third = size[:, 0:PAIRS - PAIR0], size[:, 16:20]
            link(v.tensor_scalar(evens, io128f[:, 0:PAIRS - PAIR0], 2.0, None, ALU.mult))
            link(v.tensor_scalar(evens, evens, upto[:, NE - 1:NE], None, ALU.is_lt))
            link(v.tensor_reduce(one[:, 0:1], evens, AX.X, ALU.add))
            link(v.tensor_scalar(one[:, 0:1], one[:, 0:1], float(PAIR0), None, ALU.add))
            link(v.tensor_scalar(third[:, 0:ROUNDS - ROUND0], io128f[:, ROUND0 + 1:ROUNDS + 1], float(RING), None, ALU.mult))
            link(v.tensor_scalar(third[:, 0:ROUNDS - ROUND0], third[:, 0:ROUNDS - ROUND0], one[:, 0:1], None, ALU.is_le))
            link(v.tensor_reduce(one[:, 1:2], third[:, 0:ROUNDS - ROUND0], AX.X, ALU.add))
            link(v.tensor_scalar(one[:, 1:2], one[:, 1:2], float(ROUND0), None, ALU.add))
            link(v.scalar_tensor_tensor(out=third[:, 0:1], in0=one[:, 1:2], scalar=-float(RING), in1=one[:, 0:1], op0=ALU.mult, op1=ALU.add))
            link(v.tensor_scalar(one[:, 2:4], io128f[:, 0:2], third[:, 0:1], None, ALU.is_lt))
            link(v.tensor_copy(info[:, I_PAIRS:I_PAIRS + 1], one[:, 0:1]))
            link(v.tensor_copy(info[:, I_FULL:I_REST + 2], one[:, 1:4]))
            link(v.tensor_scalar(one[:, 1:2], one[:, 1:2], -1.0, None, ALU.add))
            link(v.tensor_copy(info[:, I_PREV:I_PREV + 1], one[:, 1:2]))
            dve.sem_inc(s_info, 1)

            pairs = moe_pairs(dve)

            def x_rows(j):
                dve.wait_ge(s_xt, 2 * j + 2)
                dve.wait_ge(s_info, 1)
                v.tensor_copy(xTm[:, 4:8, :].rearrange("p k c -> p (k c)"), ps[:, 3, :]).then_inc(s_xd, 1)

            x_rows(0)
            link(v.tensor_tensor(xsel, under(upto, NEXTRA), over(io128f[:, 0:NEXTRA], NE), ALU.is_le))
            link(v.tensor_reduce(xexp, xsel, AX.X, ALU.add))
            link(v.tensor_scalar(xexp, xexp, float(NE - 1), None, ALU.min))
            link(v.tensor_copy(info[:, I_TAB + NE - TAB0:I_FULL], xexp))
            dve.sem_inc(s_xinfo, 1)
            with dve.Fori(0, pairs) as j:
                for u in range(2):
                    dve.wait_ge(s_sg[u], j + 1)
                    v.tensor_tensor(hid[u], ps[:, u, P:2 * P], sg[u], ALU.mult).then_inc(s_h[u], 1)
                dve.wait_ge(s_ht[0], j + 1)
                v.tensor_copy(hT[0], ps[:, 4, 0:P]).then_inc(s_hc[0], 1)
                x_rows(j + 1)
                dve.wait_ge(s_ht[1], j + 1)
                v.tensor_copy(hT[1], ps[:, 4, P:2 * P]).then_inc(s_hc[1], 1)

            dve.wait_ge(s_y[1], pairs)
            dve.wait_ge(s_xa, pairs + 1)
            for n in range(2 * NT):
                last = v.tensor_scalar(diag[:, n, :], ident, wgt[:, n // NT, n % NT:n % NT + 1], None, ALU.mult)
            last.then_inc(s_diag, 1)
            dve.wait_ge(s_x1d, 16 * NT)
            dve.wait_ge(s_ln2, 32)
            link(v.tensor_scalar(x[:, 0:DVE_SUMS, :], x[:, 0:DVE_SUMS, :], ALPHA, None, ALU.mult))

            def close(t):
                r = rows(t)
                dve.wait_ge(s_nrm2, t + 1)
                v.tensor_tensor(x[0:r, t, :], x[0:r, t, :], lng[0:r, :], ALU.mult).then_inc(s_g2, 1)

            for t in range(NT):
                r = rows(t)
                if t < DVE_SUMS:
                    dve.wait_ge(s_yg[t], 32)
                    for k in range(2):
                        link(v.scalar_tensor_tensor(out=x[:, t, :], in0=yg[:, t, k, :], scalar=wgt[:, k, t:t + 1], in1=x[:, t, :], op0=ALU.mult, op1=ALU.add))
                else:
                    dve.wait_ge(s_yw, t - DVE_SUMS + 1)
                    link(v.scalar_tensor_tensor(out=x[0:r, t, :], in0=x[0:r, t, :], scalar=ALPHA,
                                                in1=ps[0:r, 2 * (t % 2):2 * (t % 2) + 2, :].rearrange("p a b -> p (a b)"), op0=ALU.mult, op1=ALU.add))
                stats(t, s_mv2)
                if t:
                    close(t - 1)
                if t < NT - 1:
                    neg_mean(t, s_rstd2, t + 1)
            xt = x[0:TS, NT - 1, :]
            link(v.scalar_tensor_tensor(out=xt, in0=xt, scalar=mv[0:TS, NT - 1, 0:1], in1=lng[0:TS, :], op0=ALU.subtract, op1=ALU.mult))
            dve.wait_ge(s_rstd2, NT)
            v.scalar_tensor_tensor(out=xt, in0=xt, scalar=pw[0:TS, NT - 1:NT], in1=lnb[0:TS, :], op0=ALU.mult, op1=ALU.add).then_inc(s_last, 1)


_INS = ['x_prompt', 'x_sample', 'cache_k', 'cache_v', 'state_h', 'state_conv', 'page_table',
        'w_in', 'lambda_q1', 'lambda_k1', 'lambda_q2', 'lambda_k2', 'subln_g',
        'conv_w', 'conv_b', 'w_rg_a', 'b_rg_a', 'w_rg_x', 'b_rg_x', 'lru_lambda', 'w_out',
        'ln1_g', 'ln1_b', 'w_group_router', 'b_group_router', 'w_expert_router', 'b_expert_router',
        'w_gate_e', 'w_up_e', 'w_down_e', 'ln2_g', 'ln2_b']
_OUTS = [('y_prompt', (1, SEQ, D)), ('y_sample', (NB, SD, D)),
         ('k_prompt', (1, 1, SEQ, NH, P)), ('v_prompt', (1, 1, SEQ, NH, P)),
         ('h_prompt', (1, 1, W)), ('conv_prompt', (1, 1, 3, W)),
         ('k_sample', (1, NB, SD, NH, P)), ('v_sample', (1, NB, SD, NH, P)),
         ('h_sample', (1, NB, W)), ('conv_sample', (1, NB, 3, W))]


def kernel(**inputs):
    import numpy as _np
    import concourse.bacc as _bacc
    from concourse import mybir as _mybir
    from concourse.bass_utils import run_bass_kernel_spmd as _run

    nc = _bacc.Bacc("TRN2", target_bir_lowering=False, num_devices=1)
    arrays, ins, outs = {}, {}, {}
    for name in _INS:
        a = _np.ascontiguousarray(inputs[name])
        arrays[f"in_{name}_dram"] = a
        ins[name] = nc.dram_tensor(f"in_{name}_dram", a.shape, _mybir.dt.from_np(a.dtype), kind="ExternalInput").ap()
    for name, shape in _OUTS:
        outs[name] = nc.dram_tensor(f"out_{name}_dram", shape, _mybir.dt.float32, kind="ExternalOutput").ap()
    build(nc, ins, outs)
    r = _run(nc, [arrays], core_ids=[0])
    return tuple(r.results[0][f"out_{name}_dram"] for name, _ in _OUTS)
```
